# Optimizing a Trainium2 kernel written in Bass

```python
import math
import jax
import jax.numpy as jnp
from jax import lax
import numpy as np

D_MODEL = 1024
BATCH = 1
SEQ = 1024
DEPTH = 1
DEC_BATCH = 8
DEC_SEQ = 4
PAST_LEN = 256
PAGE_SIZE = 128

SSM_WIDTH = D_MODEL // 2
SSM_GROUP_CH = 16
N_SSM_GROUPS = SSM_WIDTH // SSM_GROUP_CH
SSM_STATE = 64
HEAD_DIM = 64
HEADS_PER_GROUP = D_MODEL // 256
WINDOWS = (128, 512, 2048)
DILATIONS = (1, 4, 16)
N_ATTN_GROUPS = len(WINDOWS)
ATTN_QKV_WIDTH = N_ATTN_GROUPS * HEADS_PER_GROUP * HEAD_DIM
ATTN_OUT_WIDTH = HEADS_PER_GROUP * HEAD_DIM
IN_PROJ_WIDTH = SSM_WIDTH + 3 * ATTN_QKV_WIDTH
N_EXPERT_GROUPS = 4
EXPERTS_PER_GROUP = 8
N_EXPERTS = N_EXPERT_GROUPS * EXPERTS_PER_GROUP
TOP_K_IN_GROUP = 2
EXPERT_FF = D_MODEL // 4
RMS_EPS = 1e-6
NEG_INF = -1e30

kernel_name = "hybrid_s5_dilated_attn_hmoe_step"

def rmsnorm(x, g):
    xf = x.astype(jnp.float32)
    xf = xf * lax.rsqrt(jnp.mean(xf * xf, axis=-1, keepdims=True) + RMS_EPS)
    return (xf * g.astype(jnp.float32)).astype(x.dtype)

def s5_scan(u, h0_re, h0_im, a_re, a_im, b_re, b_im, c_re, c_im, log_step, d_skip):
    n, t, _ = u.shape
    f32 = jnp.float32
    uf = u.astype(f32).reshape(n, t, N_SSM_GROUPS, SSM_GROUP_CH)
    lr, li = a_re.astype(f32), a_im.astype(f32)
    dt = jnp.exp(log_step.astype(f32))[:, None]
    mag = jnp.exp(lr * dt)
    ab_re, ab_im = mag * jnp.cos(li * dt), mag * jnp.sin(li * dt)
    den = lr * lr + li * li
    er, ei = ab_re - 1.0, ab_im
    f_re = (er * lr + ei * li) / den
    f_im = (ei * lr - er * li) / den
    br, bi = b_re.astype(f32), b_im.astype(f32)
    bb_re = f_re[..., None] * br - f_im[..., None] * bi
    bb_im = f_re[..., None] * bi + f_im[..., None] * br
    bu_re = jnp.einsum('ntgc,gpc->ntgp', uf, bb_re)
    bu_im = jnp.einsum('ntgc,gpc->ntgp', uf, bb_im)
    h0r, h0i = h0_re.astype(f32), h0_im.astype(f32)
    bu_re = bu_re.at[:, 0].add(ab_re * h0r - ab_im * h0i)
    bu_im = bu_im.at[:, 0].add(ab_re * h0i + ab_im * h0r)
    a_t_re = jnp.broadcast_to(ab_re, bu_re.shape)
    a_t_im = jnp.broadcast_to(ab_im, bu_im.shape)

    def combine(e1, e2):
        a1r, a1i, b1r, b1i = e1
        a2r, a2i, b2r, b2i = e2
        return (a2r * a1r - a2i * a1i, a2r * a1i + a2i * a1r,
                a2r * b1r - a2i * b1i + b2r, a2r * b1i + a2i * b1r + b2i)

    _, _, hr, hi = lax.associative_scan(combine, (a_t_re, a_t_im, bu_re, bu_im), axis=1)
    y = (jnp.einsum('ntgp,gcp->ntgc', hr, c_re.astype(f32))
         - jnp.einsum('ntgp,gcp->ntgc', hi, c_im.astype(f32)))
    y = y.reshape(n, t, SSM_WIDTH) + d_skip.astype(f32) * uf.reshape(n, t, SSM_WIDTH)
    return y, hr[:, -1], hi[:, -1]

def dilated_attn_prompt(q, k, v, dil, n_back):
    n, s, h, dh = q.shape
    f32 = jnp.float32
    length = s // dil
    nb = -(-length // n_back)
    pad = nb * n_back - length

    def by_residue(t_):
        return t_.reshape(n, length, dil, h, dh).transpose(0, 2, 1, 3, 4).astype(f32)

    qr, kr, vr = by_residue(q), by_residue(k), by_residue(v)
    qr = jnp.pad(qr, ((0, 0), (0, 0), (0, pad), (0, 0), (0, 0)))
    kr = jnp.pad(kr, ((0, 0), (0, 0), (n_back, pad), (0, 0), (0, 0)))
    vr = jnp.pad(vr, ((0, 0), (0, 0), (n_back, pad), (0, 0), (0, 0)))
    qb = qr.reshape(n, dil, nb, n_back, h, dh)
    kb = kr.reshape(n, dil, nb + 1, n_back, h, dh)
    vb = vr.reshape(n, dil, nb + 1, n_back, h, dh)
    kk = jnp.concatenate([kb[:, :, :-1], kb[:, :, 1:]], axis=3)
    vv = jnp.concatenate([vb[:, :, :-1], vb[:, :, 1:]], axis=3)
    sc = jnp.einsum('nrbqhd,nrbkhd->nrbhqk', qb, kk) * (dh ** -0.5)
    qi = jnp.arange(n_back)[:, None]
    kj = jnp.arange(2 * n_back)[None, :]
    band = (kj >= qi) & (kj <= qi + n_back)
    real = (jnp.arange(nb)[:, None, None] * n_back + kj[None]) >= n_back
    mask = band[None] & real
    sc = jnp.where(mask[:, None], sc, NEG_INF)
    m = jnp.max(sc, axis=-1, keepdims=True)
    p = jnp.exp(sc - m)
    den = jnp.sum(p, axis=-1)
    o = jnp.einsum('nrbhqk,nrbkhd->nrbqhd', p, vv) / den.transpose(0, 1, 2, 4, 3)[..., None]
    lse = m[..., 0] + jnp.log(den)
    o = o.reshape(n, dil, nb * n_back, h, dh)[:, :, :length].transpose(0, 2, 1, 3, 4).reshape(n, s, h, dh)
    lse = (lse.transpose(0, 1, 2, 4, 3).reshape(n, dil, nb * n_back, h)[:, :, :length]
           .transpose(0, 2, 1, 3).reshape(n, s, h))
    return o, lse

def dilated_attn_step(q, k_new, v_new, k_buf, v_buf, dil, n_back):
    n, t, h, dh = q.shape
    f32 = jnp.float32
    wb = k_buf.shape[1]
    kk = jnp.concatenate([k_buf, k_new], axis=1).astype(f32)
    vv = jnp.concatenate([v_buf, v_new], axis=1).astype(f32)
    idx = wb + jnp.arange(t)[:, None] - dil * jnp.arange(n_back + 1)[None, :]
    valid = idx >= 0
    idx = jnp.maximum(idx, 0)
    kg = kk[:, idx]
    vg = vv[:, idx]
    sc = jnp.einsum('nthd,ntmhd->nthm', q.astype(f32), kg) * (dh ** -0.5)
    sc = jnp.where(valid[None, :, None, :], sc, NEG_INF)
    m = jnp.max(sc, axis=-1, keepdims=True)
    p = jnp.exp(sc - m)
    den = jnp.sum(p, axis=-1)
    o = jnp.einsum('nthm,ntmhd->nthd', p, vg) / den[..., None]
    lse = m[..., 0] + jnp.log(den)
    return o, lse

def token_mixer(h, l, p, h0_re, h0_im, bufs):
    n, t, _ = h.shape
    proj = h @ p['w_in'][l]
    u = proj[..., :SSM_WIDTH]
    qkv = proj[..., SSM_WIDTH:].reshape(n, t, 3, N_ATTN_GROUPS, HEADS_PER_GROUP, HEAD_DIM)
    q, k, v = qkv[:, :, 0], qkv[:, :, 1], qkv[:, :, 2]
    y, hr, hi = s5_scan(u, h0_re, h0_im, p['ssm_a_re'][l], p['ssm_a_im'][l], p['ssm_b_re'][l],
                        p['ssm_b_im'][l], p['ssm_c_re'][l], p['ssm_c_im'][l], p['ssm_log_step'][l], p['ssm_d'][l])
    y = jax.nn.gelu(y).astype(h.dtype)
    y = y * jax.nn.sigmoid(y @ p['w_glu'][l])
    ssm_branch = y @ p['w_br_ssm'][l]
    outs, lses, new_kv = [], [], []
    for g in range(N_ATTN_GROUPS):
        dil = DILATIONS[g]
        n_back = WINDOWS[g] // dil
        qg, kg, vg = q[:, :, g], k[:, :, g], v[:, :, g]
        if bufs is None:
            o, lse = dilated_attn_prompt(qg, kg, vg, dil, n_back)
            keep = min(WINDOWS[g], t)
            new_kv += [kg[:, t - keep:], vg[:, t - keep:]]
        else:
            o, lse = dilated_attn_step(qg, kg, vg, bufs[2 * g], bufs[2 * g + 1], dil, n_back)
            new_kv += [kg, vg]
        outs.append(o)
        lses.append(lse)
    wgt = jax.nn.softmax(jnp.stack(lses, axis=0), axis=0)
    attn = jnp.sum(wgt[..., None] * jnp.stack(outs, axis=0), axis=0).reshape(n, t, ATTN_OUT_WIDTH)
    attn_branch = attn.astype(h.dtype) @ p['w_br_attn'][l]
    gates = jax.nn.sigmoid(h @ p['w_mgate'][l] + p['b_mgate'][l])
    g_ssm, g_attn = jnp.split(gates, 2, axis=-1)
    merged = g_ssm * ssm_branch + g_attn * attn_branch
    return merged @ p['w_out'][l], hr, hi, new_kv

def hier_moe(h, l, p):
    n, t, d = h.shape
    x = h.reshape(n * t, d)
    f32 = jnp.float32
    lg = (x @ p['w_router_grp'][l] + p['b_router_grp'][l]).astype(f32)
    pg = jax.nn.softmax(lg, axis=-1)
    gsel = jnp.argmax(lg, axis=-1)
    pg_sel = jnp.take_along_axis(pg, gsel[:, None], axis=-1)
    le = (x @ p['w_router_exp'][l] + p['b_router_exp'][l]).astype(f32).reshape(-1, N_EXPERT_GROUPS, EXPERTS_PER_GROUP)
    le_sel = jnp.take_along_axis(le, gsel[:, None, None], axis=1)[:, 0]
    pe = jax.nn.softmax(le_sel, axis=-1)
    w_top, e_top = lax.top_k(pe, TOP_K_IN_GROUP)
    w_top = w_top / jnp.sum(w_top, axis=-1, keepdims=True)
    eid = gsel[:, None] * EXPERTS_PER_GROUP + e_top
    combine = jnp.einsum('tk,tke->te', pg_sel * w_top, jax.nn.one_hot(eid, N_EXPERTS, dtype=f32))
    combine = combine.astype(x.dtype)
    out = jnp.zeros_like(x)
    for e in range(N_EXPERTS):
        hid = jax.nn.silu(x @ p['w_exp_gate'][l, e]) * (x @ p['w_exp_up'][l, e])
        out = out + combine[:, e:e + 1] * (hid @ p['w_exp_down'][l, e])
    return out.reshape(n, t, d)

def run_trunk(x, c, ssm_re0, ssm_im0, bufs, p):
    layer_states = []
    for l in range(DEPTH):
        mod = jax.nn.silu(c) @ p['w_ada'][l] + p['b_ada'][l]
        sh1, sc1, gt1, sh2, sc2, gt2 = jnp.split(mod[:, None, :], 6, axis=-1)
        h = rmsnorm(x, p['g_norm_mix'][l]) * (1.0 + sc1) + sh1
        lb = None if bufs is None else [b[l] for b in bufs]
        out, hr, hi, kv = token_mixer(h, l, p, ssm_re0[l], ssm_im0[l], lb)
        x = x + gt1 * out
        h = rmsnorm(x, p['g_norm_ffn'][l]) * (1.0 + sc2) + sh2
        x = x + gt2 * hier_moe(h, l, p)
        layer_states.append(kv + [hr, hi])
    y = rmsnorm(x, p['g_final'])
    n_entries = len(layer_states[0])
    new_state = [jnp.stack([layer_states[l][i] for l in range(DEPTH)], axis=0) for i in range(n_entries)]
    return y, new_state

def setup_inputs(seed: int = 0) -> dict:
    key = jax.random.key(seed)
    ks = iter(jax.random.split(key, 64))
    f32 = jnp.float32

    def nrm(shape, scale):
        return jax.random.normal(next(ks), shape, f32) * scale

    D = D_MODEL
    bufs = [min(w, PAST_LEN) for w in WINDOWS]
    kv_shape = lambda b: (DEPTH, DEC_BATCH, b, HEADS_PER_GROUP, HEAD_DIM)
    a_im0 = jnp.broadcast_to(jnp.arange(SSM_STATE, dtype=f32) * math.pi, (DEPTH, N_SSM_GROUPS, SSM_STATE))
    return {
        "x_prompt": nrm((BATCH, SEQ, D), 1.0),
        "x_sample": nrm((DEC_BATCH, DEC_SEQ, D), 1.0),
        "cache_k_w128": nrm(kv_shape(bufs[0]), 1.0),
        "cache_v_w128": nrm(kv_shape(bufs[0]), 1.0),
        "cache_k_w512": nrm(kv_shape(bufs[1]), 1.0),
        "cache_v_w512": nrm(kv_shape(bufs[1]), 1.0),
        "cache_k_w2048": nrm(kv_shape(bufs[2]), 1.0),
        "cache_v_w2048": nrm(kv_shape(bufs[2]), 1.0),
        "state_ssm_re": nrm((DEPTH, DEC_BATCH, N_SSM_GROUPS, SSM_STATE), 0.5),
        "state_ssm_im": nrm((DEPTH, DEC_BATCH, N_SSM_GROUPS, SSM_STATE), 0.5),
        "c_prompt": nrm((BATCH, D), 1.0),
        "c_sample": nrm((DEC_BATCH, D), 1.0),
        "w_ada": nrm((DEPTH, D, 6 * D), 0.5 * D ** -0.5),
        "b_ada": nrm((DEPTH, 6 * D), 0.02),
        "g_norm_mix": 1.0 + nrm((DEPTH, D), 0.01),
        "g_norm_ffn": 1.0 + nrm((DEPTH, D), 0.01),
        "g_final": 1.0 + nrm((D,), 0.01),
        "w_in": nrm((DEPTH, D, IN_PROJ_WIDTH), D ** -0.5),
        "ssm_a_re": -0.5 + nrm((DEPTH, N_SSM_GROUPS, SSM_STATE), 0.01),
        "ssm_a_im": a_im0 + nrm((DEPTH, N_SSM_GROUPS, SSM_STATE), 0.01),
        "ssm_b_re": nrm((DEPTH, N_SSM_GROUPS, SSM_STATE, SSM_GROUP_CH), (2 * SSM_GROUP_CH) ** -0.5),
        "ssm_b_im": nrm((DEPTH, N_SSM_GROUPS, SSM_STATE, SSM_GROUP_CH), (2 * SSM_GROUP_CH) ** -0.5),
        "ssm_c_re": nrm((DEPTH, N_SSM_GROUPS, SSM_GROUP_CH, SSM_STATE), (2 * SSM_STATE) ** -0.5),
        "ssm_c_im": nrm((DEPTH, N_SSM_GROUPS, SSM_GROUP_CH, SSM_STATE), (2 * SSM_STATE) ** -0.5),
        "ssm_log_step": jax.random.uniform(next(ks), (DEPTH, N_SSM_GROUPS), f32, math.log(0.001), math.log(0.1)),
        "ssm_d": nrm((DEPTH, SSM_WIDTH), 1.0),
        "w_glu": nrm((DEPTH, SSM_WIDTH, SSM_WIDTH), SSM_WIDTH ** -0.5),
        "w_br_ssm": nrm((DEPTH, SSM_WIDTH, D), SSM_WIDTH ** -0.5),
        "w_br_attn": nrm((DEPTH, ATTN_OUT_WIDTH, D), ATTN_OUT_WIDTH ** -0.5),
        "w_mgate": nrm((DEPTH, D, 2 * D), D ** -0.5),
        "b_mgate": nrm((DEPTH, 2 * D), 0.02),
        "w_out": nrm((DEPTH, D, D), D ** -0.5),
        "w_router_grp": nrm((DEPTH, D, N_EXPERT_GROUPS), D ** -0.5),
        "b_router_grp": nrm((DEPTH, N_EXPERT_GROUPS), 0.01),
        "w_router_exp": nrm((DEPTH, D, N_EXPERTS), D ** -0.5),
        "b_router_exp": nrm((DEPTH, N_EXPERTS), 0.01),
        "w_exp_gate": nrm((DEPTH, N_EXPERTS, D, EXPERT_FF), D ** -0.5),
        "w_exp_up": nrm((DEPTH, N_EXPERTS, D, EXPERT_FF), D ** -0.5),
        "w_exp_down": nrm((DEPTH, N_EXPERTS, EXPERT_FF, D), EXPERT_FF ** -0.5),
    }

def reference(x_prompt, x_sample, cache_k_w128, cache_v_w128, cache_k_w512, cache_v_w512,
              cache_k_w2048, cache_v_w2048, state_ssm_re, state_ssm_im, c_prompt, c_sample,
              w_ada, b_ada, g_norm_mix, g_norm_ffn, g_final, w_in, ssm_a_re, ssm_a_im, ssm_b_re,
              ssm_b_im, ssm_c_re, ssm_c_im, ssm_log_step, ssm_d, w_glu, w_br_ssm, w_br_attn,
              w_mgate, b_mgate, w_out, w_router_grp, b_router_grp, w_router_exp, b_router_exp,
              w_exp_gate, w_exp_up, w_exp_down):
    p = dict(w_ada=w_ada, b_ada=b_ada, g_norm_mix=g_norm_mix, g_norm_ffn=g_norm_ffn, g_final=g_final,
             w_in=w_in, ssm_a_re=ssm_a_re, ssm_a_im=ssm_a_im, ssm_b_re=ssm_b_re, ssm_b_im=ssm_b_im,
             ssm_c_re=ssm_c_re, ssm_c_im=ssm_c_im, ssm_log_step=ssm_log_step, ssm_d=ssm_d, w_glu=w_glu,
             w_br_ssm=w_br_ssm, w_br_attn=w_br_attn, w_mgate=w_mgate, b_mgate=b_mgate, w_out=w_out,
             w_router_grp=w_router_grp, b_router_grp=b_router_grp, w_router_exp=w_router_exp,
             b_router_exp=b_router_exp, w_exp_gate=w_exp_gate, w_exp_up=w_exp_up, w_exp_down=w_exp_down)
    zeros_state = jnp.zeros((DEPTH, x_prompt.shape[0], N_SSM_GROUPS, SSM_STATE), jnp.float32)
    y_prompt, pstate = run_trunk(x_prompt, c_prompt, zeros_state, zeros_state, None, p)
    sample_bufs = [cache_k_w128, cache_v_w128, cache_k_w512, cache_v_w512, cache_k_w2048, cache_v_w2048]
    y_sample, sstate = run_trunk(x_sample, c_sample, state_ssm_re, state_ssm_im, sample_bufs, p)
    pk128, pv128, pk512, pv512, pk2048, pv2048, p_re, p_im = pstate
    sk128, sv128, sk512, sv512, sk2048, sv2048, s_re, s_im = sstate
    return (y_prompt, y_sample, pk128, pv128, pk512, pv512, pk2048, pv2048, p_re, p_im,
            sk128, sv128, sk512, sv512, sk2048, sv2048, s_re, s_im)


_drawn_inputs = setup_inputs


def setup_inputs(seed=0):
    import zlib

    import numpy as np

    out = dict(_drawn_inputs(seed))
    spreads = {}
    factors = {'cache_k_w128': 3.583,
     'cache_v_w128': 3.14,
     'cache_k_w512': 3.865,
     'cache_v_w512': 3.477,
     'cache_k_w2048': 8.0,
     'cache_v_w2048': 8.0,
     'g_norm_mix': 5.959,
     'g_norm_ffn': 4.136,
     'g_final': 5.714,
     'ssm_a_re': 3.731,
     'ssm_c_im': 2.779,
     'b_mgate': 8.0,
     'b_router_grp': 5.881,
     'b_router_exp': 8.0}
    for name, (base, spread) in spreads.items():
        noise = np.random.default_rng([zlib.crc32(name.encode()), seed]).standard_normal(out[name].shape)
        drawn = base * np.exp(spread * noise) if base else spread * noise
        out[name] = jnp.asarray(drawn.astype(out[name].dtype))
    for name, factor in factors.items():
        out[name] = (out[name] * factor).astype(out[name].dtype)
    return out
```

```python
import math
from contextlib import ExitStack

import numpy as np

import concourse.bass as bass
from concourse import mybir

ALU = mybir.AluOpType
ACT = mybir.ActivationFunctionType
AX = mybir.AxisListType
F32 = mybir.dt.float32
I32 = mybir.dt.int32
U32 = mybir.dt.uint32

P = 128
D = 1024
KT = D // P
SEQ = 1024
DEC_B, DEC_T = 8, 4
NS = DEC_B * DEC_T
N = SEQ + NS
TT = SEQ // P
NT = TT + 1
CH = 3
CW = N // CH
HEADS, HD = 4, 64
GROUPS = 3
DIL = (1, 4, 16)
WIN = (128, 512, 2048)
PAST = 256
SSM_W, SSM_G, SSM_C, SSM_S = 512, 32, 16, 64
SP2 = SSM_G // 2
L = 8
NCH = SEQ // L
NE, NG, EPG, FF = 32, 4, 8, 256
NBLK = NE + 2 * N // P
MIN_TURNS = (-(-2 * N // P) - 1) // 2
EPS = 1e-6
NEG = -1e30
RING = 4
WB = 256


def rows_of(t):
    return P if t < TT else NS


class Counted:

    def __init__(self, sem):
        self.sem, self.n = sem, 0

    def step(self, eng, ins):
        self.n += 1
        ins.then_inc(self.sem, 1)
        eng.wait_ge(self.sem, self.n)


def build(nc, I, O, scratch):
    ctx = ExitStack()
    with ctx:
        def sb(name, shape, dt=F32, stack=ctx):
            return stack.enter_context(nc.sbuf_tensor(name, shape, dt))

        front_sems = []

        def sem(name):
            if front_sems is not None:
                s = nc.alloc_semaphore(name)
                front_sems.append(s)
                return s
            return ctx.enter_context(nc.semaphore(name))

        ident = sb("ident", [P, P])
        band_mask = sb("band_mask", [P, 2 * P])
        pair_mask = sb("pair_mask", [P, P])
        dec_mask = [sb(f"dec_mask{g}", [P, (128, 256, 64)[g] + NS]) for g in range(GROUPS)]
        mod_t = sb("mod_t", [P, 6 * KT, 1 + DEC_B])
        prm_t = sb("prm_t", [P, 80])
        gain1 = sb("gain1", [P, KT, 1 + DEC_B])
        q_new = sb("q_new", [P, 6, NS])
        k_new = sb("k_new", [P, 6, NS])
        v_new = sb("v_new", [NS, 3 * WB])
        h_t = sb("h_t", [P, KT * N])
        ring = sb("ring", [P, RING, KT * WB])
        u_rows = sb("u_rows", [P, SSM_G, L, SSM_C])
        big = sb("big", [P, 19584])
        q_t = big[:, 0:6336].rearrange("p (c n) -> p c n", c=6)
        k_t = big[:, 6336:12672].rearrange("p (c n) -> p c n", c=6)
        v_rows = big[:, 12672:18816].rearrange("p (g t c) -> p g t c", g=GROUPS, t=TT)
        ht3 = h_t[:, :].rearrange("p (k n) -> p k n", k=KT)
        psum = ctx.enter_context(nc.psum_tensor("psum", [P, 8, 512], F32))
        bank = [psum[:, i, :] for i in range(8)]

        def token_cols(g, t, view):
            if g == 0:
                return view[:, t * P:(t + 1) * P]
            if g == 1:
                r, b = t % 4, t // 4
                return view[:, 512 * b + r:512 * (b + 1):4]
            return view[:, t:SEQ:8]

        w_in, w_ada = I["w_in"][0], I["w_ada"][0]
        ada_blk = [("ada", b) for b in range(24)]
        in_blk = [("q", b) for b in range(3)] + [("k", b) for b in range(3)] + [("u", b) for b in range(2)] + [("v", b) for b in range(3)]
        order = ada_blk[:8]
        rest = ada_blk[8:]
        for n, b in enumerate(in_blk):
            order += [b] + rest[:2]
            rest = rest[2:]
        order += rest
        IN_COL = {"u": 0, "q": SSM_W, "k": SSM_W + 768, "v": SSM_W + 1536}

        def block_src(kind, b):
            w, c = (w_ada, b * WB) if kind == "ada" else (w_in, IN_COL[kind] + b * WB)
            return w[:, c:c + WB].rearrange("(k p) c -> p k c", p=P)

        units = [("x", t, hf) for t in range(NT) for hf in range(2)]
        first_unit, last_unit = {}, {}
        for blk in order:
            first_unit[blk] = len(units)
            kind, b = blk
            if kind in "qk":
                units += [(kind, 2 * b + c, n) for c in range(2) for n in range(CH)]
            elif kind in "uv":
                units += [(kind, b, t) for t in range(NT)]
            last_unit[blk] = len(units)
        NB = 6
        owner = ["dve" if (e % 2 == 0 or u == ("x", TT, 1)) else "act" for e, u in enumerate(units)]

        def evac_count(e):
            return sum(1 for i in range(e + 1) if owner[i] == owner[e])

        s_id, s_small, s_xrow = sem("identity_ready"), sem("small_loaded"), [sem(f"x_rows_loaded{i}") for i in range(2)]
        s_iota = sem("iota_ready")
        s_w = [sem(f"weights{i}_loaded") for i in range(RING)]
        s_unit, s_ev = sem("unit_in_psum"), {"dve": sem("unit_copied_dve"), "act": sem("unit_copied_act")}
        s_ada, s_ac, s_adt, s_modv = (sem("ada_block_in_psum"), sem("ada_block_copied"), sem("ada_rows_turned"),
                                      sem("modulation_ready"))
        s_ct, s_cv = sem("cond_transposed"), sem("cond_copied")
        s_sig, s_silu, s_ssq, s_ms, s_sqrt, s_xn = (sem("cond_sigmoid"), sem("cond_silu"), sem("square_sums"),
                                                     sem("mean_square"), sem("root_ready"), sem("x_normed"))
        s_dve1, s_act1, s_pool1 = sem("dve_chain1"), sem("act_chain1"), sem("pool_chain1")
        s_kt, s_kt_ev = sem("k_rows_in_psum"), sem("k_rows_copied")
        s_us = sem("u_sample_stored")
        s_ksl = sem("k_rows_stored")

        with ExitStack() as st:
            rows = sb("x_rows", [P, 768], stack=st)
            ada_rows = sb("ada_rows", [P, 4 * D], stack=st)
            c_rows, c_sig = ada_rows[0:1 + DEC_B, 0:D], ada_rows[0:1 + DEC_B, D:2 * D]
            quad = sb("quad", [P, 1 + DEC_B], stack=st)
            c_t = sb("c_t", [P, KT, 32], stack=st)
            p_rows = sb("p_rows", [80, P], stack=st)
            sq = sb("sq", [P, D], stack=st)
            ssq = sb("ssq", [P, NT], stack=st)
            rstd = sb("rstd", [P, NT], stack=st)
            iq = sb("iq", [P, 256], I32, stack=st)
            ip = sb("ip", [P, 4], I32, stack=st)
            fq = sb("fq", [P, 4, 256], stack=st)
            fp = sb("fp", [P, 4], stack=st)
            tmpm = sb("tmpm", [P, 256], stack=st)
            u_s = sb("u_s", [NS, SSM_W], stack=st)
            krow = sb("krow", [P, 2, WB], stack=st)
            xr = big[:, 19584 - NT * D:19584].rearrange("p (t d) -> p t d", t=NT)
            del rows

            k_jobs = [(g, t) for g in range(GROUPS) for t in range(NT)
                      if t == TT or t >= TT - min(WIN[g], SEQ) // P]

            job_at = {last_unit[("k", 2)] + 3 + 2 * n: n for n in range(len(k_jobs))}

            def ada_bank(b):
                return bank[5 if b < 8 and b % 2 else 7][:, 0:WB]

            with nc.Block() as block:
                @block.sync
                def _(sp):
                    sp.dma_start(c_rows[0:1, :], I["c_prompt"]).then_inc(s_small, 16)
                    sp.dma_start(c_rows[1:1 + DEC_B, :], I["c_sample"]).then_inc(s_small, 16)
                    sp.dma_start(p_rows[0:48, :], I["b_ada"][0].rearrange("(r c) -> r c", c=P)).then_inc(s_small, 16)
                    sp.dma_start(p_rows[48:56, :], I["g_norm_mix"][0].rearrange("(r c) -> r c", c=P)).then_inc(s_small, 16)
                    sp.dma_start(p_rows[56:64, :], I["g_norm_ffn"][0].rearrange("(r c) -> r c", c=P)).then_inc(s_small, 16)
                    sp.dma_start(p_rows[64:80, :], I["b_mgate"][0].rearrange("(r c) -> r c", c=P)).then_inc(s_small, 16)
                    for n, blk in enumerate(order):
                        if n >= RING:
                            old = order[n - RING]
                            if old[0] == "ada":
                                sp.wait_ge(s_ada, old[1] + 1)
                            else:
                                sp.wait_ge(s_unit, last_unit[old])
                        sp.dma_start(ring[:, n % RING, :].rearrange("p (k c) -> p k c", k=KT),
                                     block_src(*blk)).then_inc(s_w[n % RING], 16)
                        if n in (0, 1):
                            sp.dma_start(xr[:, 4 * n:4 * n + 4, :],
                                         I["x_prompt"][0, 4 * n * P:4 * (n + 1) * P].rearrange("(t p) d -> p t d", p=P)).then_inc(s_xrow[n], 16)
                        if n == 1:
                            sp.dma_start(xr[0:NS, TT, :], I["x_sample"].rearrange("b t d -> (b t) d")).then_inc(s_xrow[n], 16)

                    for w in range(2):
                        e = units.index(("u", w, TT))
                        sp.wait_ge(s_ev[owner[e]], evac_count(e))
                    sp.dma_start(scratch["u_new"], u_s[:, :]).then_inc(s_us, 16)
                    sp.wait_ge(s_us, 16)

                @block.gpsimd
                def _(pool):
                    c = Counted(s_pool1)
                    c.step(pool, nc.gpsimd.memset(ident[:, :], 0.0))
                    nc.gpsimd.affine_select(out=ident[:, :], in_=ident[:, :], compare_op=ALU.not_equal, fill=1.0,
                                            base=0, pattern=[[-1, P]], channel_multiplier=1).then_inc(s_id, 1)
                    nc.gpsimd.iota(iq[:, :], pattern=[[1, 256]], base=0, channel_multiplier=0).then_inc(s_iota, 1)
                    nc.gpsimd.iota(ip[:, 0:1], pattern=[[0, 1]], base=0, channel_multiplier=1).then_inc(s_iota, 1)
                    out_k = {0: "k0", 1: "k1", 2: "k2"}
                    for n, (g, t) in enumerate(k_jobs):
                        pool.wait_ge(s_kt_ev, n + 1)
                        if t < TT:
                            lo = t - (TT - min(WIN[g], SEQ) // P)
                            dst = O["p" + out_k[g]][0, 0].rearrange("s h d -> s (h d)")[lo * P:(lo + 1) * P, :]
                            pool.dma_start(dst, krow[:, n % 2, :]).then_inc(s_ksl, 16)
                        else:
                            dst = O["s" + out_k[g]][0].rearrange("b t h d -> (b t) (h d)")
                            pool.dma_start(dst, krow[0:NS, n % 2, :]).then_inc(s_ksl, 16)
                        pool.wait_ge(s_ksl, 16 * (n + 1))
                @block.tensor
                def _(pe):
                    pe.wait_ge(s_id, 1)
                    pe.wait_ge(s_small, 96)
                    pe.wait_ge(s_silu, 1)
                    for k in range(KT):
                        nc.tensor.transpose(bank[0][:, 16 * k:16 * k + 9], c_rows[:, k * P:(k + 1) * P],
                                            ident[0:9, 0:9])
                    nc.tensor.transpose(bank[0][:, 256:336], p_rows[:, :], ident[0:80, 0:80]).then_inc(s_ct, 1)
                    pe.wait_ge(s_cv, 2)

                    def ada(n, b):
                        pe.wait_ge(s_w[n % RING], 16 * (n // RING + 1))
                        w = ring[:, n % RING, :].rearrange("p (k c) -> p k c", k=KT)
                        if b >= 2:
                            pe.wait_ge(s_ac, b - 1 if b < 8 else b)
                        for k in range(KT):
                            m = nc.tensor.matmul(ada_bank(b)[32 * (k % 4):32 * (k % 4) + 32, :], c_t[:, k, :], w[:, k, :],
                                                 start=(k < 4), stop=(k >= 4))
                        m.then_inc(s_ada, 1)

                    def turn_ada(tiles, copied):
                        pe.wait_ge(s_ac, copied)
                        for i in range(tiles):
                            m = nc.tensor.matmul(bank[6][:, 9 * i:9 * i + 9], ada_rows[:, i * P:(i + 1) * P], quad[:, :], start=True, stop=True)
                        m.then_inc(s_adt, 1)

                    def bank_free(e):
                        if e >= NB:
                            pe.wait_ge(s_ev[owner[e - NB]], evac_count(e - NB))

                    for n in range(8):
                        ada(n, n)
                    turn_ada(16, 8)
                    e = 0
                    for t in range(NT):
                        pe.wait_ge(s_xn, t + 1)
                        for hf in range(2):
                            bank_free(e)
                            r = rows_of(t)
                            for k in range(4):
                                m = nc.tensor.transpose(bank[e % NB][:, k * P:k * P + r],
                                                        xr[0:r, t, (4 * hf + k) * P:(4 * hf + k + 1) * P],
                                                        ident[0:r, 0:r])
                            m.then_inc(s_unit, 1)
                            e += 1
                    for e0 in range(2 * NT - 2, 2 * NT):
                        pe.wait_ge(s_ev[owner[e0]], evac_count(e0))
                    for e0 in range(2 * NT - 4, 2 * NT - 2):
                        pe.wait_ge(s_ev[owner[e0]], evac_count(e0))

                    def turn_k(m0):
                        g, t = k_jobs[m0]
                        if m0 == 0:
                            for e0 in range(last_unit[("k", 2)] - 2, last_unit[("k", 2)]):
                                pe.wait_ge(s_ev[owner[e0]], evac_count(e0))
                        else:
                            pe.wait_ge(s_kt_ev, m0)
                        r = rows_of(t)
                        for c in range(2):
                            m = nc.tensor.transpose(bank[6][0:r, c * P:(c + 1) * P],
                                                    k_t[:, 2 * g + c, t * P:t * P + r], ident[:, :])
                        m.then_inc(s_kt, 1)

                    for n in range(8, len(order)):
                        kind, b = order[n]
                        if kind == "ada":
                            ada(n, b)
                            continue
                        pe.wait_ge(s_w[n % RING], 16 * (n // RING + 1))
                        w = ring[:, n % RING, :].rearrange("p (k c) -> p k c", k=KT)
                        if kind in "qk":
                            for c in range(2):
                                for j in range(CH):
                                    bank_free(e + j)
                                for k in range(KT):
                                    for j in range(CH):
                                        m = nc.tensor.matmul(bank[(e + j) % NB][:, 0:CW], w[:, k, c * P:(c + 1) * P],
                                                             ht3[:, k, j * CW:(j + 1) * CW],
                                                             start=(k == 0), stop=(k == KT - 1))
                                        if k == KT - 1:
                                            m.then_inc(s_unit, 1)
                                e += CH
                        else:
                            for t in range(NT):
                                if e in job_at:
                                    turn_k(job_at[e])
                                bank_free(e)
                                for k in range(KT):
                                    if t == TT:
                                        lhs = ht3[:, k, SEQ:N]
                                    elif kind == "u":
                                        lhs = ht3[:, k, t:SEQ:L]
                                    else:
                                        lhs = token_cols(b, t, ht3[:, k, :])
                                    m = nc.tensor.matmul(bank[e % NB][0:rows_of(t), 0:WB], lhs, w[:, k, :],
                                                         start=(k == 0), stop=(k == KT - 1))
                                m.then_inc(s_unit, 1)
                                e += 1
                    pe.wait_ge(s_kt_ev, len(k_jobs))
                    turn_ada(32, 24)

                def copy_unit(e, u, eng, nceng):
                    kind, a, b = u
                    src = bank[e % NB]
                    s = s_ev[owner[e]]
                    dve = owner[e] == "dve"

                    def copy(dst, view):
                        if dve:
                            return nc.vector.tensor_copy(dst, view)
                        return nc.scalar.activation(dst, view, ACT.Copy)

                    if kind in "qk":
                        dst = q_t if kind == "q" else k_t
                        copy(dst[:, a, b * CW:(b + 1) * CW], src[:, 0:CW]).then_inc(s, 1)
                    elif kind == "u":
                        if b == TT:
                            copy(u_s[:, a * WB:(a + 1) * WB], src[0:NS, 0:WB]).then_inc(s, 1)
                        else:
                            copy(u_rows[:, 16 * a:16 * a + 16, b, :],
                                 src[:, 0:WB].rearrange("p (g c) -> p g c", c=SSM_C)).then_inc(s, 1)
                    elif b == TT:
                        copy(v_new[:, a * WB:(a + 1) * WB], src[0:NS, 0:WB]).then_inc(s, 1)
                    else:
                        copy(v_rows[:, a, b, :], src[:, 0:WB]).then_inc(s, 1)

                @block.scalar
                def _(act):
                    c = Counted(s_act1)
                    act.wait_ge(s_small, 96)
                    nc.scalar.activation(c_sig[:, :], c_rows[:, :], ACT.Sigmoid).then_inc(s_sig, 1)
                    act.wait_ge(s_dve1, 1)
                    for t in range(NT):
                        r = rows_of(t)
                        if t == 0:
                            act.wait_ge(s_xrow[0], 16)
                        if t == 4:
                            act.wait_ge(s_xrow[1], 32)
                        c.step(act, nc.scalar.activation(sq[0:r, :], xr[0:r, t, :], ACT.Square,
                                                         accum_out=ssq[0:r, t:t + 1]))
                    act.sem_inc(s_ssq, 1)
                    act.wait_ge(s_ms, 1)
                    nc.scalar.activation(rstd[:, :], ssq[:, :], ACT.Sqrt).then_inc(s_sqrt, 1)
                    act.wait_ge(s_modv, 1)
                    for e, u in enumerate(units):
                        if owner[e] != "act":
                            continue
                        act.wait_ge(s_unit, e + 1)
                        if u[0] == "x":
                            _, t, hf = u
                            for k in range(4):
                                kk = 4 * hf + k
                                m = nc.scalar.activation(ht3[:, kk, t * P:(t + 1) * P],
                                                         bank[e % NB][:, k * P:(k + 1) * P], ACT.Identity,
                                                         bias=mod_t[:, kk, 0:1], scale=gain1[:, kk, 0:1])
                            m.then_inc(s_ev["act"], 1)
                        else:
                            copy_unit(e, u, act, nc.scalar)

                @block.vector
                def _(dve):
                    c = Counted(s_dve1)
                    V = nc.vector
                    c.step(dve, V.memset(ssq[:, :], 1.0))
                    c.step(dve, V.memset(c_t[:, :, :], 0.0))
                    dve.wait_ge(s_id, 1)
                    c.step(dve, V.tensor_tensor(quad[:, :], ident[:, 0:9], ident[:, 32:41], ALU.add))
                    for i in (64, 96):
                        c.step(dve, V.tensor_tensor(quad[:, :], quad[:, :], ident[:, i:i + 9], ALU.add))
                    dve.wait_ge(s_sig, 1)
                    V.tensor_tensor(c_rows[:, :], c_rows[:, :], c_sig[:, :], ALU.mult).then_inc(s_silu, 1)
                    dve.wait_ge(s_ct, 1)
                    V.tensor_copy(c_t[:, :, 0:9], bank[0][:, 0:P].rearrange("p (k c) -> p k c", c=16)[:, :, 0:9]).then_inc(s_cv, 1)
                    V.tensor_copy(prm_t[:, :], bank[0][:, 256:336]).then_inc(s_cv, 1)

                    def copy_ada(b):
                        dve.wait_ge(s_ada, b + 1)
                        if b == 8:
                            dve.wait_ge(s_adt, 1)
                        V.tensor_copy(ada_rows[:, (b if b < 8 else b - 8) * WB:(b + 1 if b < 8 else b - 7) * WB],
                                      ada_bank(b)).then_inc(s_ac, 1)

                    for b in range(5):
                        copy_ada(b)
                    dve.wait_ge(s_ssq, 1)
                    V.tensor_scalar(ssq[:, :], ssq[:, :], 1.0 / D, EPS, ALU.mult, ALU.add).then_inc(s_ms, 1)
                    dve.wait_ge(s_sqrt, 1)
                    c.step(dve, V.reciprocal(rstd[:, :], rstd[:, :]))
                    for t in range(NT):
                        r = rows_of(t)
                        V.tensor_scalar(xr[0:r, t, :], xr[0:r, t, :], rstd[0:r, t:t + 1], None, ALU.mult).then_inc(s_xn, 1)
                    for b in range(5, 8):
                        copy_ada(b)
                    dve.wait_ge(s_adt, 1)
                    dve.wait_ge(s_cv, 2)
                    c.step(dve, V.tensor_tensor(mod_t[:, 0:16, :], bank[6][:, 0:144].rearrange("p (k c) -> p k c", c=9),
                                                prm_t[:, 0:16].unsqueeze(2).to_broadcast([P, 16, 9]), ALU.add))
                    c.step(dve, V.tensor_scalar(gain1[:, :, :], mod_t[:, 8:16, :], 1.0, None, ALU.add))
                    c.step(dve, V.tensor_tensor(gain1[:, :, :], gain1[:, :, :],
                                                prm_t[:, 48:56].unsqueeze(2).to_broadcast([P, KT, 9]), ALU.mult))
                    dve.sem_inc(s_modv, 1)
                    def build_masks():
                        dve.wait_ge(s_iota, 2)
                        c.step(dve, V.tensor_copy(fq[:, 0, :], iq[:, :]))
                        c.step(dve, V.tensor_copy(fp[:, 0:1], ip[:, 0:1]))
                        c.step(dve, V.tensor_scalar(ip[:, 1:2], ip[:, 0:1], 3, None, ALU.bitwise_and))
                        c.step(dve, V.tensor_copy(fp[:, 1:2], ip[:, 1:2]))
                        c.step(dve, V.tensor_scalar(ip[:, 2:3], ip[:, 0:1], 31, 2, ALU.bitwise_and, ALU.logical_shift_right))
                        c.step(dve, V.tensor_copy(fp[:, 2:3], ip[:, 2:3]))
                        c.step(dve, V.tensor_scalar(ip[:, 3:4], ip[:, 0:1], 1, None, ALU.bitwise_and))
                        c.step(dve, V.tensor_copy(fp[:, 3:4], ip[:, 3:4]))
                        for k, (a, b, o0, o1) in enumerate(((3, None, ALU.bitwise_and, None),
                                                            (31, 2, ALU.bitwise_and, ALU.logical_shift_right),
                                                            (1, None, ALU.bitwise_and, None))):
                            if o1 is None:
                                c.step(dve, V.tensor_scalar(tmpm[:, :].bitcast(I32), iq[:, :], a, None, o0))
                            else:
                                c.step(dve, V.tensor_scalar(tmpm[:, :].bitcast(I32), iq[:, :], a, b, o0, o1))
                            c.step(dve, V.tensor_copy(fq[:, 1 + k, :], tmpm[:, :].bitcast(I32)))
                        J, J4, JN, J2 = (fq[:, k, :] for k in range(4))

                        def additive(dst, w):
                            c.step(dve, V.tensor_scalar(dst, tmpm[:, 0:w], -1.0, -NEG, ALU.add, ALU.mult))

                        c.step(dve, V.tensor_scalar(tmpm[:, 0:P], J[:, 0:P], fp[:, 0:1], None, ALU.is_ge))
                        additive(band_mask[:, 0:P], P)
                        c.step(dve, V.tensor_scalar(tmpm[:, 0:P], J[:, 0:P], fp[:, 0:1], None, ALU.is_le))
                        additive(band_mask[:, P:2 * P], P)
                        c.step(dve, V.scalar_tensor_tensor(out=tmpm[:, 0:P], in0=J2[:, 0:P], scalar=fp[:, 3:4],
                                                           in1=tmpm[:, 0:P], op0=ALU.is_equal, op1=ALU.mult))
                        additive(pair_mask[:, :], P)
                        c.step(dve, V.tensor_scalar(tmpm[:, 0:P], J[:, 0:P], fp[:, 1:2], None, ALU.is_ge))
                        additive(dec_mask[0][:, 0:128], 128)
                        c.step(dve, V.tensor_scalar(tmpm[:, :], J4, fp[:, 1:2], None, ALU.is_equal))
                        additive(dec_mask[1][:, 0:256], 256)
                        additive(dec_mask[2][:, 0:64], 64)
                        for g in range(GROUPS):
                            op, w = (ALU.is_le if g == 0 else ALU.is_equal), (128, 256, 64)[g]
                            c.step(dve, V.tensor_scalar(tmpm[:, 0:NS], J4[:, 0:NS], fp[:, 1:2], None, op))
                            c.step(dve, V.scalar_tensor_tensor(out=tmpm[:, 0:NS], in0=JN[:, 0:NS], scalar=fp[:, 2:3],
                                                               in1=tmpm[:, 0:NS], op0=ALU.is_equal, op1=ALU.mult))
                            additive(dec_mask[g][:, w:w + NS], NS)

                    def copy_k(n):
                        dve.wait_ge(s_kt, n + 1)
                        if n >= 2:
                            dve.wait_ge(s_ksl, 16 * (n - 1))
                        r = rows_of(k_jobs[n][1])
                        V.tensor_copy(krow[0:r, n % 2, :], bank[6][0:r, 0:WB]).then_inc(s_kt_ev, 1)

                    for e, u in enumerate(units):
                        if u[0] != "x" and units[e - 1][0] == "x":
                            build_masks()
                        for b in range(8, 24):
                            if first_unit[("ada", b)] == e:
                                copy_ada(b)
                        if e in job_at:
                            copy_k(job_at[e])
                        if owner[e] != "dve":
                            continue
                        dve.wait_ge(s_unit, e + 1)
                        if u[0] == "x":
                            _, t, hf = u
                            if t < TT:
                                for k in range(4):
                                    kk = 4 * hf + k
                                    m = V.tensor_scalar(ht3[:, kk, t * P:(t + 1) * P], bank[e % NB][:, k * P:(k + 1) * P],
                                                        gain1[:, kk, 0:1], mod_t[:, kk, 0:1], ALU.mult, ALU.add)
                                m.then_inc(s_ev["dve"], 1)
                            else:
                                for k in range(4):
                                    kk = 4 * hf + k
                                    dst = ht3[:, kk, SEQ:N].rearrange("p (b t) -> p b t", t=DEC_T)
                                    src = bank[e % NB][:, k * P:k * P + NS].rearrange("p (b t) -> p b t", t=DEC_T)
                                    c.step(dve, V.tensor_tensor(dst, src, gain1[:, kk, 1:9].unsqueeze(2).to_broadcast([P, DEC_B, DEC_T]), ALU.mult))
                                    m = V.tensor_tensor(dst, dst, mod_t[:, kk, 1:9].unsqueeze(2).to_broadcast([P, DEC_B, DEC_T]), ALU.add)
                                m.then_inc(s_ev["dve"], 1)
                        else:
                            copy_unit(e, u, dve, V)
                    for b in range(8, 24):
                        if first_unit[("ada", b)] == len(units):
                            copy_ada(b)
                    dve.wait_ge(s_adt, 2)
                    V.tensor_tensor(mod_t[:, 16:48, :], bank[6][:, 0:288].rearrange("p (k c) -> p k c", c=9),
                                    prm_t[:, 16:48].unsqueeze(2).to_broadcast([P, 32, 9]), ALU.add).then_inc(s_modv, 1)
                    for e0 in (len(units) - 1, len(units) - 2):
                        dve.wait_ge(s_ev[owner[e0]], evac_count(e0))
                    V.tensor_copy(q_new[:, :, :], q_t[:, :, SEQ:N]).then_inc(s_modv, 1)
                    V.tensor_copy(k_new[:, :, :], k_t[:, :, SEQ:N]).then_inc(s_modv, 1)

        att = [(g, t) for g in range(GROUPS) for t in range(TT)]
        has_prev = [(g == 0 and t >= 1) or (g == 1 and t >= 4) for g, t in att]
        nkb = [2 if h else 1 for h in has_prev]
        kb_before = [sum(nkb[:u]) for u in range(len(att) + 1)]
        NU = len(att)

        def place(rows, g, t):
            if g == 0:
                return rows[t * P:(t + 1) * P]
            if g == 1:
                return rows[512 * (t // 4) + t % 4:512 * (t // 4 + 1):4]
            return rows[t:SEQ:8]

        OB = 4
        s_sc, s_msk, s_nm, s_p = sem("scores_in_psum"), sem("scores_masked"), sem("row_max_ready"), sem("probs_ready")
        s_gw = [sem(f"gate_weights{i}_loaded") for i in range(2)]
        s_zr, s_zst, s_vst = sem("zero_rows_ready"), sem("zero_rows_stored"), sem("v_stored")
        s_pt, s_pta, s_ptd = sem("probs_t_in_psum"), sem("probs_t_copied_act"), sem("probs_t_copied_dve")
        s_pv, s_o, s_st = sem("values_in_psum"), sem("values_copied"), [sem(f"att_rows_stored{i}") for i in range(OB)]

        def wait_pt_copied(eng, x):
            eng.wait_ge(s_pta if x % 2 == 0 else s_ptd, x // 2 + 1)

        with ExitStack() as st:
            s_sb = sb("s_sb", [P, 2, HEADS, 2 * P], stack=st)
            p_sb = sb("p_sb", [P, 2, HEADS, 2 * P], stack=st)
            pt_sb = sb("pt_sb", [P, 2, 2, HEADS, P], stack=st)
            o_sb = sb("o_sb", [P, OB, HEADS, HD + 2], stack=st)

            with nc.Block() as block:
                @block.gpsimd
                def _(pool):
                    zeros = ring[:, 3, 0:D]
                    nc.gpsimd.memset(zeros, 0.0).then_inc(s_zr, 1)
                    pool.wait_ge(s_zr, 1)
                    for b in range(2 + 2 * MIN_TURNS, NBLK, 2):
                        pool.wait_ge(s_pv, (b - 2 * MIN_TURNS) * NU // NBLK)
                        pool.dma_start(scratch["expert_rows"][b * P:(b + 2) * P, :].rearrange("(b p) d -> p b d", p=P),
                                       zeros.unsqueeze(1).to_broadcast([P, 2, D])).then_inc(s_zst, 16)
                    total = 0
                    for g in range(GROUPS):
                        for t in range(TT):
                            dst = O[f"pv{g}"][0, 0].rearrange("s h d -> s (h d)")
                            if g == 0:
                                if t != TT - 1:
                                    continue
                            elif g == 1:
                                if t < 4:
                                    continue
                                dst = dst.rearrange("(i r) c -> r i c", r=4)[t % 4]
                            else:
                                dst = dst.rearrange("(i r) c -> r i c", r=8)[t]
                            pool.dma_start(dst, v_rows[:, g, t, :]).then_inc(s_vst, 16)
                            total += 1
                        dst = O[f"sv{g}"][0].rearrange("b t h d -> (b t) (h d)")
                        pool.dma_start(dst, v_new[:, g * WB:(g + 1) * WB]).then_inc(s_vst, 16)
                        total += 1
                    pool.wait_ge(s_vst, 16 * total)
                    pool.wait_ge(s_zst, 16 * (NBLK // 2 - 1 - MIN_TURNS))

                @block.tensor
                def _(pe):
                    def scores(u):
                        g, t = att[u]
                        if u >= 2:
                            pe.wait_ge(s_msk, u - 1)
                        for h in range(HEADS):
                            par, k2 = h % 2, h // 2
                            lo = HD * par
                            q = token_cols(g, t, q_t[lo:lo + HD, 2 * g + k2, :])
                            kk = k_t[lo:lo + HD, 2 * g + k2, :]
                            if not has_prev[u]:
                                keys, w = token_cols(g, t, kk), P
                            elif g == 0:
                                keys, w = kk[:, (t - 1) * P:(t + 1) * P], 2 * P
                            else:
                                keys, w = kk[:, t % 4:SEQ:4], 2 * P
                            m = nc.tensor.matmul(psum[:, 2 * (u % 2) + par, 256 * k2:256 * k2 + w], q, keys,
                                                 start=True, stop=True)
                        m.then_inc(s_sc, 1)

                    def turn_probs(u):
                        pe.wait_ge(s_p, u + 1)
                        for kb in range(nkb[u]):
                            x = kb_before[u] + kb
                            if x >= 2:
                                wait_pt_copied(pe, x - 2)
                            for s in range(HEADS):
                                m = nc.tensor.transpose(bank[4 + x % 2][:, s * P:(s + 1) * P],
                                                        p_sb[:, u % 2, s, kb * P:(kb + 1) * P], ident[:, :])
                            m.then_inc(s_pt, 1)

                    def values(u):
                        g, t = att[u]
                        if u >= 2:
                            pe.wait_ge(s_o, u - 1)
                        for kb in range(nkb[u]):
                            wait_pt_copied(pe, kb_before[u] + kb)
                        prev = t - 1 if g == 0 else t - 4
                        for h in range(HEADS):
                            slot = 2 * (h % 2) + h // 2
                            for kb in range(nkb[u]):
                                tile = t if kb == nkb[u] - 1 else prev
                                m = nc.tensor.matmul(bank[6 + u % 2][:, h * HD:(h + 1) * HD], pt_sb[:, u % 2, kb, slot, :],
                                                     v_rows[:, g, tile, h * HD:(h + 1) * HD],
                                                     start=(kb == 0), stop=(kb == nkb[u] - 1))
                        m.then_inc(s_pv, 1)

                    for i in range(NU + 2):
                        if i < NU:
                            scores(i)
                        if i >= 2:
                            values(i - 2)
                        if 1 <= i <= NU:
                            turn_probs(i - 1)

                @block.vector
                def _(dve):
                    V = nc.vector
                    for i in range(NU + 1):
                        if i < NU:
                            g, t = att[i]
                            w = nkb[i] * P
                            mask = band_mask[:, 2 * P - w:2 * P] if g < 2 else pair_mask[:, :]
                            dve.wait_ge(s_sc, i + 1)
                            if i >= 2:
                                dve.wait_ge(s_p, i - 1)
                            pair = psum[:, 2 * (i % 2):2 * (i % 2) + 2, :].rearrange("p b (s c) -> p (b s) c", s=2)
                            V.scalar_tensor_tensor(out=s_sb[:, i % 2, :, 0:w], in0=pair[:, :, 0:w], scalar=HD ** -0.5,
                                                   in1=mask.unsqueeze(1).to_broadcast([P, HEADS, w]),
                                                   op0=ALU.mult, op1=ALU.add).then_inc(s_msk, 1)
                            dve.wait_ge(s_msk, i + 1)
                            if i >= OB:
                                dve.wait_ge(s_st[i % OB], 16 * (i // OB))
                            V.tensor_reduce(o_sb[:, i % OB, :, HD].rearrange("p (k r) -> p r k", r=2),
                                            s_sb[:, i % 2, :, 0:w], AX.X, ALU.max, negate=True).then_inc(s_nm, 1)
                        if i >= 1:
                            for x in range(kb_before[i - 1], kb_before[i]):
                                if x % 2 == 1:
                                    dve.wait_ge(s_pt, x + 1)
                                    if i >= 3:
                                        dve.wait_ge(s_pv, i - 2)
                                    V.tensor_copy(pt_sb[:, (i - 1) % 2, x - kb_before[i - 1], :, :],
                                                  bank[5].rearrange("p (s c) -> p s c", s=HEADS)).then_inc(s_ptd, 1)

                @block.scalar
                def _(act):
                    A = nc.scalar
                    for i in range(NU + 2):
                        if i < NU:
                            w = nkb[i] * P
                            act.wait_ge(s_nm, i + 1)
                            if i >= 2:
                                act.wait_ge(s_pt, kb_before[i - 1])
                            for s in range(HEADS):
                                h = 2 * (s % 2) + s // 2
                                m = A.activation(p_sb[:, i % 2, s, 0:w], s_sb[:, i % 2, s, 0:w], ACT.Exp,
                                                 bias=o_sb[:, i % OB, h, HD:HD + 1], scale=1.0,
                                                 accum_out=o_sb[:, i % OB, h, HD + 1:HD + 2])
                            m.then_inc(s_p, 1)
                        if 1 <= i <= NU:
                            for x in range(kb_before[i - 1], kb_before[i]):
                                if x % 2 == 0:
                                    act.wait_ge(s_pt, x + 1)
                                    if i >= 3:
                                        act.wait_ge(s_pv, i - 2)
                                    A.activation(pt_sb[:, (i - 1) % 2, x - kb_before[i - 1], :, :],
                                                 bank[4].rearrange("p (s c) -> p s c", s=HEADS), ACT.Copy).then_inc(s_pta, 1)
                        if i >= 2:
                            u = i - 2
                            act.wait_ge(s_pv, u + 1)
                            A.activation(o_sb[:, u % OB, :, 0:HD], bank[6 + u % 2][:, 0:WB].rearrange("p (h d) -> p h d", h=HEADS),
                                         ACT.Copy).then_inc(s_o, 1)

                @block.sync
                def _(sp):
                    for b in range(2):
                        sp.dma_start(ring[:, b, :].rearrange("p (k c) -> p k c", k=KT),
                                     I["w_mgate"][0][:, b * WB:(b + 1) * WB].rearrange("(k p) c -> p k c", p=P)).then_inc(s_gw[b], 16)
                    for u, (g, t) in enumerate(att):
                        sp.wait_ge(s_o, u + 1)
                        sp.wait_ge(s_p, u + 1)
                        dst = place(scratch["att_rows"].rearrange("n g h d -> n g (h d)")[:, g, :], g, t)
                        sp.dma_start(dst, o_sb[:, u % OB, :, :].rearrange("p h d -> p (h d)")).then_inc(s_st[u % OB], 16)
                    for i in range(OB):
                        sp.wait_ge(s_st[i], 16 * NU // OB)

        attn_t = big[:, 0:2112].rearrange("p (c n) -> p c n", c=2)
        y_t = big[:, 10720:14944].rearrange("p (c n) -> p c n", c=4)
        y_rows = u_rows[:, :, :, :].rearrange("p g j c -> p (g j c)").rearrange("p (i n r c) -> p i n r c", i=L, n=SP2, r=2)
        ring_f = ring[:, :, :].rearrange("p s c -> p (s c)")
        NV = NCH + 1 + DEC_B
        v_re = big[:, 6336:6336 + SP2 * NV].rearrange("p (n c) -> p n c", n=SP2)
        v_im = big[:, 8528:8528 + SP2 * NV].rearrange("p (n c) -> p n c", n=SP2)
        v_both = big[:, 6336:6336 + 2 * SP2 * NV].rearrange("p (i n c) -> p i n c", i=2, n=SP2)
        us = big[0:16, 6336:6336 + 4096].rearrange("p (g j c) -> p g j c", g=SSM_G, j=L)
        e_re, e_im, t_re, t_im = (big[:, 10720 + 2048 * i:12768 + 2048 * i].rearrange("p (n c) -> p n c", n=SP2) for i in range(4))
        g_all = big[0:SSM_C, 14816:18912].rearrange("p (g c) -> p g c", g=SSM_G)
        ys = ring_f[0:DEC_B, 4096:6144].rearrange("p (i n r c) -> p i n r c", i=DEC_T, n=SP2, r=2)
        ca_re = big[:, 2112:4160].rearrange("p (n i c) -> p n i c", n=SP2, i=L)
        ca_im = big[:, 4160:6208].rearrange("p (n i c) -> p n i c", n=SP2, i=L)
        ba_re = ring_f[:, 4096:6144].rearrange("p (n i c) -> p n i c", n=SP2, i=L)
        ba_im = ring_f[:, 6144:8192].rearrange("p (n i c) -> p n i c", n=SP2, i=L)
        toe = ring_f[:, 0:4096].rearrange("p (g c) -> p g c", g=SSM_G)
        y2_t = big[:, 6336:10560].rearrange("p (c n) -> p c n", c=4)
        TWO_PI = 2 * math.pi
        PI1 = 6.28125
        PI2 = float(np.float32(np.round((TWO_PI - PI1) * 2 ** 20) / 2 ** 20))
        PI3 = TWO_PI - PI1 - PI2
        ROUND = 1.5 * 2 ** 23

        GB = 3
        FILL = {"start": 2, "params": 2, "c_h0": 9, "merge": 6, "merged": 8}
        for g in range(GROUPS):
            FILL.update({f"scores{g}": 1, f"turn_scores{g}": 1, f"turn_probs{g}": 2, f"values{g}": 1, f"rows{g}": 1, f"next{g}": 1})
        GATE_UNITS = 2 * KT * CH
        DK = (128, 256, 64)
        KB = (1, 2, 1)
        KP = (128, 128, 64)
        s_kc, s_vc = [sem(f"cache_k{g}_loaded") for g in range(GROUPS)], [sem(f"cache_v{g}_loaded") for g in range(GROUPS)]
        s_ktp, s_kte = sem("cache_k_t_in_psum"), sem("cache_k_t_copied")
        s_stp, s_ste = sem("new_scores_t_in_psum"), sem("new_scores_t_copied")
        s_sp, s_sm, s_nx, s_pe, s_ptp, s_pte = (sem("new_scores_in_psum"), sem("new_scores_masked"), sem("new_max_ready"),
                                                sem("new_probs_ready"), sem("new_probs_t_in_psum"), sem("new_probs_t_copied"))
        s_op, s_oa, s_os, s_orp, s_or, s_ost = (sem("new_values_t_in_psum"), sem("new_values_a"), sem("new_values_t_ready"),
                                                sem("new_rows_in_psum"), sem("new_rows_copied"), sem("new_rows_stored"))
        s_clr, s_all, s_dif, s_ex, s_mrg = (sem("merge_cleared"), sem("merge_rows_loaded"), sem("max_differences"),
                                            sem("max_factors"), sem("merged"))
        s_atp, s_ate = sem("attn_t_in_psum"), sem("attn_t_copied")
        s_dve3, s_pool3 = sem("dve_chain3"), sem("pool_chain3")
        s_pl, s_bl, s_cl, s_hl = sem("ssm_params_loaded"), sem("ssm_b_loaded"), sem("ssm_c_loaded"), sem("ssm_h0_loaded")
        s_dtr, s_pt4, s_ct4 = sem("step_rows_ready"), sem("params_in_psum"), sem("c_in_psum")
        s_a1, s_a2, s_a3, s_a4 = sem("dt_ready"), sem("exponents_ready"), sem("magnitudes_ready"), sem("angles_ready")
        s_a5 = sem("sines_ready")
        s_pw, s_cah, s_ca = sem("powers_ready"), sem("c_ready"), sem("ca_ready")
        s_qp = sem("query_pairs_ready")
        s_gu, s_gc, s_gst = sem("gate_unit_in_psum"), sem("gate_unit_ready"), [sem(f"gate_unit_stored{i}") for i in range(GB)]
        kt_banks = [(g, i) for g in range(GROUPS) for i in range(8 * 2 * DK[g] // 512)]
        kt_before = [sum(1 for b in kt_banks if b[0] < g) for g in range(GROUPS + 1)]

        st34 = ExitStack()
        pc = sb("ssm_pc", [P, 48], stack=st34)
        sm = sb("ssm_small", [P, 16, SP2], stack=st34)
        bb = sb("b_bar", [P, 2, SP2, SSM_C], stack=st34)
        cc = sb("c_cols", [P, 2, SP2, SSM_C], stack=st34)
        pw = sb("powers", [P, 2, L + 1, SP2], stack=st34)
        tp = sb("tmp_pow", [P, 256], stack=st34)
        h0 = sb("h0_cols", [P, 2, SP2, DEC_B], stack=st34)
        with ExitStack() as st:
            tmp_e = big[:, 0:1024].rearrange("p (n c) -> p n c", n=SP2)
            b_raw = big[:, 1024:1536].rearrange("p (i n c) -> p i n c", i=2, n=SP2)
            rp = big[:, 1536:1792].rearrange("p (i j n) -> p i j n", i=2, j=L)
            par_rows = big[0:48, 1792:1920]
            ls = big[0:48, 1920:1922]
            h_rows4 = big[:, 10432:10688].rearrange("p (a c) -> p a c", a=2)
            c_rows4 = big[:, 18912:19424].rearrange("p (a c) -> p a c", a=4)
            g_sb = sb("gate_units", [P, GB, CW], stack=st)
            vc = sb("vc", [P, 4096], stack=st)
            st_sb = sb("st_sb", [P, 3, P], stack=st)
            s2 = sb("s2", [P, 288], stack=st)
            p2 = s2
            pt2 = sb("pt2", [P, 3, P], stack=st)
            q_pair = sb("q_pair", [P, 6, 2, NS], stack=st)
            o2 = sb("o2", [HD, P], stack=st)
            d_sb = sb("d_sb", [P, HD + 2], stack=st)
            kc = big[:, 6336:10432]
            kct = big[:, 14816:18912]
            kcv, vcv = ([x[0:KP[g], 0:8 * KB[g] * WB].rearrange("p (n b c) -> p n b c", n=8, b=KB[g]) for g in range(GROUPS)]
                        for x in (kc, vc))
            attn_rows = vc[:, 0:NT * WB].rearrange("p (t c) -> p t c", t=NT)
            MERGE = ((kct, 0, 5), (kc, 5, NT))
            merge = [x[:, 0:(t1 - t0) * 792].rearrange("p (t g h d) -> p t g h d", t=t1 - t0, g=GROUPS, h=HEADS) for x, t0, t1 in MERGE]
            small = [sb(f"merge_small{i}", [P, NT, GROUPS, HEADS], stack=st) for i in range(2)]
            tot = [sb(f"merge_tot{i}", [P, NT, HEADS], stack=st) for i in range(2)]
            caches = [("cache_k_w128", "cache_v_w128"), ("cache_k_w512", "cache_v_w512"), ("cache_k_w2048", "cache_v_w2048")]

            with nc.Block() as block:
                @block.sync
                def _(sp):
                    def load_cache(src, dst, s, g):
                        rows = src[0].rearrange("n s h d -> n s (h d)")
                        if g < 2:
                            for b in range(KB[g]):
                                sp.dma_start(dst[:, :, b, :], rows[:, b * P:(b + 1) * P, :].rearrange("n s c -> s n c")).then_inc(s, 16)
                        else:
                            for a in range(16):
                                sp.dma_start(dst[4 * a:4 * a + 4, :, 0, :],
                                             rows[:, 16 * a:16 * a + 4, :].rearrange("n s c -> s n c")).then_inc(s, 16)

                    sp.dma_start(par_rows[0:16, :], I["ssm_a_re"][0].rearrange("(n r) s -> n (r s)", r=2)).then_inc(s_pl, 16)
                    sp.dma_start(par_rows[16:32, :], I["ssm_a_im"][0].rearrange("(n r) s -> n (r s)", r=2)).then_inc(s_pl, 16)
                    sp.dma_start(ls[32:48, :], I["ssm_log_step"][0].rearrange("(n r) -> n r", r=2)).then_inc(s_pl, 16)
                    for i, nm_ in enumerate(("ssm_b_re", "ssm_b_im")):
                        for r in range(2):
                            sp.dma_start(b_raw[64 * r:64 * r + 64, i, :, :],
                                         I[nm_][0].rearrange("(n r) s c -> r s n c", r=2)[r]).then_inc(s_bl, 16)
                    for i, nm_ in enumerate(("ssm_c_re", "ssm_c_im")):
                        for n in range(SP2):
                            sp.dma_start(c_rows4[16 * (n % 8):16 * (n % 8) + 16, 2 * i + n // 8, :].rearrange("c (r s) -> c r s", r=2),
                                         I[nm_][0, 2 * n:2 * n + 2].rearrange("r c s -> c r s")).then_inc(s_cl, 16)
                    for i, nm_ in enumerate(("state_ssm_re", "state_ssm_im")):
                        sp.dma_start(h_rows4[:, i, :], I[nm_][0].rearrange("b (n r) s -> (b n) (r s)", r=2)).then_inc(s_hl, 16)
                    for g in range(GROUPS):
                        if g:
                            sp.wait_ge(s_ktp, kt_before[g])
                        load_cache(I[caches[g][0]], kcv[g], s_kc[g], g)
                        if g:
                            sp.wait_ge(s_op, g)
                        load_cache(I[caches[g][1]], vcv[g], s_vc[g], g)
                        if g:
                            sp.wait_ge(s_or, g)
                            for h in range(HEADS):
                                sp.dma_start(scratch["att_rows"][SEQ:N, g - 1, h, :], d_sb[h * NS:(h + 1) * NS, :]).then_inc(s_ost, 16)
                    sp.wait_ge(s_or, GROUPS)
                    for h in range(HEADS):
                        sp.dma_start(scratch["att_rows"][SEQ:N, GROUPS - 1, h, :], d_sb[h * NS:(h + 1) * NS, :]).then_inc(s_ost, 16)
                    sp.wait_ge(s_clr, 1)
                    for m_, (_, t0, t1) in zip(merge, MERGE):
                        t1 = min(t1, TT)
                        sp.dma_start(m_[:, 0:t1 - t0].rearrange("p t g h d -> p t (g h d)"),
                                     scratch["att_rows"][t0 * P:t1 * P].rearrange("(t p) g h d -> p t (g h d)", p=P)).then_inc(s_all, 16)
                    sp.wait_ge(s_ost, 64 * GROUPS)
                    sp.dma_start(merge[1][0:NS, TT - 5].rearrange("p g h d -> p (g h d)"),
                                 scratch["att_rows"][SEQ:N].rearrange("n g h d -> n (g h d)")).then_inc(s_all, 16)
                    for i in range(GB):
                        sp.wait_ge(s_gst[i], 16 * (GATE_UNITS // GB))

                @block.gpsimd
                def _(pool):
                    G = nc.gpsimd
                    c = Counted(s_pool3)
                    pool.wait_ge(s_pw, 1)
                    pool.wait_ge(s_cah, 1)
                    sh = [P, SP2, L, SSM_C]
                    pr = pw[:, 0, 1:L + 1, :].rearrange("p i n -> p n i").unsqueeze(3).to_broadcast(sh)
                    pi = pw[:, 1, 1:L + 1, :].rearrange("p i n -> p n i").unsqueeze(3).to_broadcast(sh)
                    cr, nci = (cc[:, i, :, :].unsqueeze(2).to_broadcast(sh) for i in range(2))
                    tmp = e_im.rearrange("p n (i c) -> p n i c", i=L)
                    c.step(pool, G.tensor_tensor(ca_re, cr, pr, ALU.mult))
                    c.step(pool, G.tensor_tensor(tmp, nci, pi, ALU.mult))
                    c.step(pool, G.tensor_tensor(ca_re, ca_re, tmp, ALU.add))
                    c.step(pool, G.tensor_tensor(ca_im, cr, pi, ALU.mult))
                    c.step(pool, G.tensor_tensor(tmp, nci, pr, ALU.mult))
                    G.tensor_tensor(ca_im, tmp, ca_im, ALU.subtract).then_inc(s_ca, 1)

                @block.tensor
                def _(pe):
                    T_ = nc.tensor
                    done = [0]

                    def fill(step):
                        for u in range(done[0], done[0] + FILL[step]):
                            b, c0, j = u // 6, u // 3 % 2 * P, u % 3
                            pe.wait_ge(s_gw[b % 2], 16 * (b // 2 + 1))
                            if u >= 4:
                                pe.wait_ge(s_gc, u - 3)
                            w_ = ring[:, b % 2, :].rearrange("p (k c) -> p k c", k=KT)
                            for k in range(KT):
                                m = T_.matmul(bank[4 + u % 4][:, 0:CW], w_[:, k, c0:c0 + P], ht3[:, k, j * CW:(j + 1) * CW],
                                              start=(k == 0), stop=(k == KT - 1))
                            m.then_inc(s_gu, 1)
                        done[0] += FILL[step]

                    fill("start")
                    pe.wait_ge(s_dtr, 1)
                    T_.transpose(bank[3][:, 0:48], par_rows[:, :], ident[0:48, 0:48]).then_inc(s_pt4, 1)
                    fill("params")
                    pe.wait_ge(s_cl, 32 * SP2)
                    pe.wait_ge(s_hl, 32)
                    for i in range(4):
                        m = T_.transpose(bank[0][:, i * P:(i + 1) * P], c_rows4[:, i, :], ident[:, :])
                    for i in range(2):
                        m = T_.transpose(bank[1][:, i * P:(i + 1) * P], h_rows4[:, i, :], ident[:, :])
                    m.then_inc(s_ct4, 1)
                    fill("c_h0")
                    pe.wait_ge(s_cah, 1)
                    pe.wait_ge(s_a1, 1)
                    for g in range(GROUPS):
                        w = KP[g]
                        pe.wait_ge(s_kc[g], 16 * (KB[g] if g < 2 else 16))
                        for i in range(kt_before[g], kt_before[g + 1]):
                            if i >= 2:
                                pe.wait_ge(s_kte, i - 1)
                            for j in range(512 // w):
                                piece = (i - kt_before[g]) * (512 // w) + j
                                nn, hp, b = piece // (2 * KB[g]), piece // KB[g] % 2, piece % KB[g]
                                m = nc.tensor.transpose(bank[i % 2][:, j * w:(j + 1) * w], kcv[g][:, nn, b, hp * P:(hp + 1) * P],
                                                        ident[0:w, 0:w])
                            m.then_inc(s_ktp, 1)
                        pe.wait_ge(s_kte, kt_before[g + 1])
                        if g:
                            pe.wait_ge(s_or, g)
                        fill(f"scores{g}")
                        kv = kct[:, 0:8 * 2 * DK[g]].rearrange("p (n r k) -> p n r k", n=8, r=2)
                        if g == 0:
                            pe.wait_ge(s_qp, 1)
                        for hp in range(2):
                            for nn in range(DEC_B):
                                for b in range(KB[g]):
                                    o = bank[2][0:w, b * P + hp * 64:b * P + hp * 64 + 64].rearrange("p (r n) -> p r n", r=2)
                                    nc.tensor.matmul(o[:, :, 4 * nn:4 * nn + 4], kv[:, nn, hp, b * w:(b + 1) * w],
                                                     q_pair[:, 2 * g + hp, :, 4 * nn:4 * nn + 4], start=True, stop=True)
                            m = nc.tensor.matmul(bank[2][0:NS, 256 + hp * 64:256 + hp * 64 + 64], k_new[:, 2 * g + hp, :],
                                                 q_pair[:, 2 * g + hp, :, :].rearrange("p r n -> p (r n)"), start=True, stop=True)
                        m.then_inc(s_stp, 1)
                        fill(f"turn_scores{g}")
                        pe.wait_ge(s_ste, g + 1)
                        for b in range(KB[g]):
                            nc.tensor.transpose(bank[0][:, b * P:b * P + w], st_sb[0:w, b, :], ident[0:w, 0:w])
                        nc.tensor.transpose(bank[0][:, DK[g]:DK[g] + NS], st_sb[0:NS, 2, :], ident[0:NS, 0:NS]).then_inc(s_sp, 1)
                        fill(f"turn_probs{g}")
                        pe.wait_ge(s_pe, g + 1)
                        for b in range(KB[g]):
                            nc.tensor.transpose(bank[1][0:w, b * P:(b + 1) * P], p2[:, b * P:b * P + w], ident[:, :])
                        nc.tensor.transpose(bank[1][0:NS, 256:256 + P], p2[:, DK[g]:DK[g] + NS], ident[:, :]).then_inc(s_ptp, 1)
                        fill(f"values{g}")
                        pe.wait_ge(s_pte, g + 1)
                        pe.wait_ge(s_vc[g], 16 * (KB[g] if g < 2 else 16))
                        for h in range(HEADS):
                            for nn in range(DEC_B):
                                c0 = h * NS + 4 * nn
                                for b in range(KB[g]):
                                    nc.tensor.matmul(bank[2][0:HD, c0:c0 + 4], vcv[g][:, nn, b, h * HD:(h + 1) * HD],
                                                     pt2[0:w, b, c0:c0 + 4], start=(b == 0), stop=(b == KB[g] - 1))
                            m = nc.tensor.matmul(bank[3][0:HD, h * NS:(h + 1) * NS], v_new[:, g * WB + h * HD:g * WB + (h + 1) * HD],
                                                 pt2[0:NS, 2, h * NS:(h + 1) * NS], start=True, stop=True)
                        m.then_inc(s_op, 1)
                        fill(f"rows{g}")
                        pe.wait_ge(s_os, g + 1)
                        nc.tensor.transpose(bank[3][:, 256:256 + HD], o2[:, :], ident[0:HD, 0:HD]).then_inc(s_orp, 1)
                        fill(f"next{g}")
                    fill("merge")
                    fill("merged")
                    pe.wait_ge(s_mrg, 1)
                    pe.wait_ge(s_or, GROUPS)
                    for t in range(NT):
                        if t >= 2:
                            pe.wait_ge(s_ate, t - 1)
                        r = rows_of(t)
                        for c in range(2):
                            m = nc.tensor.transpose(bank[t % 2][:, c * P:c * P + r], attn_rows[0:r, t, c * P:(c + 1) * P], ident[0:r, 0:r])
                        m.then_inc(s_atp, 1)

                @block.vector
                def _(dve):
                    V = nc.vector
                    c = Counted(s_dve3)

                    def tt(out, a, b, op):
                        c.step(dve, V.tensor_tensor(out, a, b, op))

                    def cmul(o_re, o_im, a_re_, a_im_, b_re_, b_im_, tmp):
                        tt(o_re, a_re_, b_re_, ALU.mult)
                        tt(tmp, a_im_, b_im_, ALU.mult)
                        tt(o_re, o_re, tmp, ALU.subtract)
                        tt(o_im, a_re_, b_im_, ALU.mult)
                        tt(tmp, a_im_, b_re_, ALU.mult)
                        tt(o_im, o_im, tmp, ALU.add)

                    dve.wait_ge(s_pl, 48)
                    V.tensor_copy(par_rows[32:48, :].rearrange("p (r s) -> p r s", r=2),
                                  ls[32:48, :].unsqueeze(2).to_broadcast([16, 2, SSM_S])).then_inc(s_dtr, 1)
                    dve.wait_ge(s_pt4, 1)
                    V.tensor_copy(pc[:, :], bank[3][:, 0:48]).then_inc(s_a1, 1)
                    dve.wait_ge(s_a2, 1)
                    dve.wait_ge(s_a1, 1)
                    lr, li, dt = pc[:, 0:16], pc[:, 16:32], sm[:, 2, :]
                    tt(sm[:, 3, :], lr, dt, ALU.mult)
                    tt(sm[:, 4, :], li, dt, ALU.mult)
                    dve.sem_inc(s_a3, 1)
                    c.step(dve, V.tensor_scalar(sm[:, 0, :], sm[:, 4, :], 1.0 / TWO_PI, ROUND, ALU.mult, ALU.add))
                    c.step(dve, V.tensor_scalar(sm[:, 0, :], sm[:, 0, :], -ROUND, None, ALU.add))
                    for part in (PI1, PI2, PI3):
                        c.step(dve, V.scalar_tensor_tensor(out=sm[:, 4, :], in0=sm[:, 0, :], scalar=-part, in1=sm[:, 4, :],
                                                           op0=ALU.mult, op1=ALU.add))
                    c.step(dve, V.tensor_scalar(sm[:, 4, :], sm[:, 4, :], 3.1415925, -3.1415925, ALU.min, ALU.max))
                    c.step(dve, V.scalar_tensor_tensor(out=sm[:, 9, :], in0=sm[:, 4, :], scalar=-1.0, in1=sm[:, 4, :],
                                                       op0=ALU.mult, op1=ALU.max))
                    c.step(dve, V.tensor_scalar(sm[:, 9, :], sm[:, 9, :], -1.0, math.pi / 2, ALU.mult, ALU.add))
                    dve.sem_inc(s_a3, 1)
                    dve.wait_ge(s_ct4, 1)
                    c.step(dve, V.tensor_copy(cc[:, 0, :, :], bank[0][:, 0:256].rearrange("p (n c) -> p n c", c=SSM_C)))
                    c.step(dve, V.tensor_scalar(cc[:, 1, :, :], bank[0][:, 256:512].rearrange("p (n c) -> p n c", c=SSM_C), -1.0, None, ALU.mult))
                    c.step(dve, V.tensor_copy(h0[:, 0], bank[1][:, 0:P].rearrange("p (b n) -> p n b", n=SP2)))
                    c.step(dve, V.tensor_copy(h0[:, 1], bank[1][:, P:2 * P].rearrange("p (b n) -> p n b", n=SP2)))
                    dve.sem_inc(s_cah, 1)
                    dve.wait_ge(s_a5, 2)
                    dve.wait_ge(s_a4, 2)
                    co, si, mag = sm[:, 7, :], sm[:, 8, :], sm[:, 5, :]
                    c.step(dve, V.memset(pw[:, 0, 0, :], 1.0))
                    c.step(dve, V.memset(pw[:, 1, 0, :], 0.0))
                    tt(pw[:, 0, 1, :], mag, co, ALU.mult)
                    tt(pw[:, 1, 1, :], mag, si, ALU.mult)

                    def power(k, lo, hi, n):
                        sh = [P, n, SP2]
                        t_ = tp[:, 0:n * SP2].rearrange("p (k n) -> p k n", k=n)
                        cmul(pw[:, 0, lo:hi, :], pw[:, 1, lo:hi, :], pw[:, 0, 1:1 + n, :], pw[:, 1, 1:1 + n, :],
                             pw[:, 0, k, :].unsqueeze(1).to_broadcast(sh), pw[:, 1, k, :].unsqueeze(1).to_broadcast(sh), t_)

                    power(1, 2, 3, 1)
                    power(2, 3, 5, 2)
                    power(4, 5, 9, 4)
                    dve.sem_inc(s_pw, 1)
                    for j in range(L):
                        c.step(dve, V.tensor_copy(rp[:, :, j, :], pw[:, :, L - 1 - j, :]))
                    a_re_, a_im_ = pw[:, 0, 1, :], pw[:, 1, 1, :]
                    er, fr, fi, den, tm = sm[:, 10, :], sm[:, 11, :], sm[:, 12, :], sm[:, 13, :], sm[:, 14, :]
                    c.step(dve, V.tensor_scalar(er, a_re_, -1.0, None, ALU.add))
                    tt(den, lr, lr, ALU.mult)
                    tt(tm, li, li, ALU.mult)
                    tt(den, den, tm, ALU.add)
                    c.step(dve, V.reciprocal(den, den))
                    tt(fr, er, lr, ALU.mult)
                    tt(tm, a_im_, li, ALU.mult)
                    tt(fr, fr, tm, ALU.add)
                    tt(fr, fr, den, ALU.mult)
                    tt(fi, a_im_, lr, ALU.mult)
                    tt(tm, er, li, ALU.mult)
                    tt(fi, fi, tm, ALU.subtract)
                    tt(fi, fi, den, ALU.mult)
                    dve.wait_ge(s_bl, 64)
                    sh = [P, SP2, SSM_C]
                    t_ = tp[:, 0:256].rearrange("p (n c) -> p n c", c=SSM_C)
                    cmul(bb[:, 0], bb[:, 1], fr.unsqueeze(2).to_broadcast(sh), fi.unsqueeze(2).to_broadcast(sh),
                         b_raw[:, 0], b_raw[:, 1], t_)
                    sh = [P, SP2, L, SSM_C]
                    tmp4 = e_re.rearrange("p n (i c) -> p n i c", i=L)
                    cmul(ba_re, ba_im, rp[:, 0].rearrange("p i n -> p n i").unsqueeze(3).to_broadcast(sh),
                         rp[:, 1].rearrange("p i n -> p n i").unsqueeze(3).to_broadcast(sh),
                         bb[:, 0].unsqueeze(2).to_broadcast(sh), bb[:, 1].unsqueeze(2).to_broadcast(sh), tmp4)
                    c.step(dve, V.memset(q_pair[:, :, :, :], 0.0))
                    V.tensor_copy(q_pair[0:HD, :, 0, :], q_new[0:HD, :, :])
                    V.tensor_copy(q_pair[HD:P, :, 1, :], q_new[HD:P, :, :]).then_inc(s_qp, 1)
                    for g in range(GROUPS):
                        w = KP[g]
                        for i in range(kt_before[g], kt_before[g + 1]):
                            dve.wait_ge(s_ktp, i + 1)
                            if g and i == kt_before[g]:
                                dve.wait_ge(s_stp, g)
                            V.tensor_copy(kct[:, (i - kt_before[g]) * 512:(i - kt_before[g] + 1) * 512], bank[i % 2]).then_inc(s_kte, 1)
                        dve.wait_ge(s_stp, g + 1)
                        if g:
                            dve.wait_ge(s_sp, g)
                        V.tensor_copy(st_sb[0:w, 0:KB[g], :], bank[2][0:w, 0:KB[g] * P].rearrange("p (b c) -> p b c", b=KB[g]))
                        V.tensor_copy(st_sb[0:NS, 2, :], bank[2][0:NS, 256:384]).then_inc(s_ste, 1)
                        dve.wait_ge(s_sp, g + 1)
                        wd = DK[g] + NS
                        V.scalar_tensor_tensor(out=s2[:, 0:wd], in0=bank[0][:, 0:wd], scalar=HD ** -0.5, in1=dec_mask[g][:, :],
                                               op0=ALU.mult, op1=ALU.add).then_inc(s_sm, 1)
                        dve.wait_ge(s_sm, g + 1)
                        if g:
                            dve.wait_ge(s_ost, 64 * g)
                        V.tensor_reduce(d_sb[:, HD:HD + 1], s2[:, 0:wd], AX.X, ALU.max, negate=True).then_inc(s_nx, 1)
                        dve.wait_ge(s_ptp, g + 1)
                        V.tensor_copy(pt2[0:w, 0:KB[g], :], bank[1][0:w, 0:KB[g] * P].rearrange("p (b c) -> p b c", c=P))
                        V.tensor_copy(pt2[0:NS, 2, :], bank[1][0:NS, 256:384]).then_inc(s_pte, 1)
                        dve.wait_ge(s_oa, g + 1)
                        V.tensor_tensor(o2[:, :], o2[:, :], bank[3][0:HD, 0:P], ALU.add).then_inc(s_os, 1)
                        dve.wait_ge(s_orp, g + 1)
                        V.tensor_copy(d_sb[:, 0:HD], bank[3][:, 256:256 + HD]).then_inc(s_or, 1)
                    V.memset(merge[1][:, TT - 5].rearrange("p g h d -> p (g h d)"), 1.0).then_inc(s_clr, 1)
                    k = 0
                    src = (co, si)
                    for _ in range(3):
                        dst = (sm[:, k, :], sm[:, 14 + k, :])
                        tt(dst[0], src[0], src[0], ALU.mult)
                        tt(tp[:, 0:16], src[1], src[1], ALU.mult)
                        tt(dst[0], dst[0], tp[:, 0:16], ALU.subtract)
                        c.step(dve, V.scalar_tensor_tensor(out=dst[1], in0=src[0], scalar=2.0, in1=src[1], op0=ALU.mult, op1=ALU.mult))
                        src, k = dst, 1 - k
                    dve.wait_ge(s_ca, 1)
                    c.step(dve, V.memset(e_re[:, :, 0], 1.0))
                    c.step(dve, V.memset(e_im[:, :, 0], 0.0))
                    w = 1
                    while w < NCH:
                        sh = [P, SP2, w]
                        cmul(e_re[:, :, w:2 * w], e_im[:, :, w:2 * w], e_re[:, :, 0:w], e_im[:, :, 0:w],
                             src[0].unsqueeze(2).to_broadcast(sh), src[1].unsqueeze(2).to_broadcast(sh), tmp_e[:, :, 0:w])
                        w *= 2
                        if w < NCH:
                            dst = (sm[:, k, :], sm[:, 14 + k, :])
                            tt(dst[0], src[0], src[0], ALU.mult)
                            tt(tp[:, 0:16], src[1], src[1], ALU.mult)
                            tt(dst[0], dst[0], tp[:, 0:16], ALU.subtract)
                            c.step(dve, V.scalar_tensor_tensor(out=dst[1], in0=src[0], scalar=2.0, in1=src[1], op0=ALU.mult, op1=ALU.mult))
                            src, k = dst, 1 - k
                    dve.wait_ge(s_all, 48)
                    lo, tm = tot[0], tot[1]
                    for m_, (_, t0, t1) in zip(merge, MERGE):
                        nm = m_[:, :, :, :, HD]
                        c.step(dve, V.tensor_reduce(lo[:, t0:t1, :], nm.rearrange("p t g h -> p t h g"), AX.X, ALU.min))
                        c.step(dve, V.tensor_tensor(small[0][:, t0:t1], nm, lo[:, t0:t1, :].unsqueeze(2).to_broadcast([P, t1 - t0, GROUPS, HEADS]),
                                                    ALU.subtract))
                    dve.sem_inc(s_dif, 1)
                    dve.wait_ge(s_ex, 1)
                    for m_, (_, t0, t1) in zip(merge, MERGE):
                        c.step(dve, V.tensor_tensor(small[0][:, t0:t1], small[1][:, t0:t1], m_[:, :, :, :, HD + 1], ALU.mult))
                    c.step(dve, V.tensor_reduce(tm[:, :, :], small[0][:, :, :, :].rearrange("p t g h -> p t h g"), AX.X, ALU.add))
                    c.step(dve, V.reciprocal(tm[:, :, :], tm[:, :, :]))
                    c.step(dve, V.tensor_tensor(small[0][:, :, :, :], small[1][:, :, :, :],
                                                tm[:, :, :].unsqueeze(2).to_broadcast([P, NT, GROUPS, HEADS]), ALU.mult))
                    for m_, (_, t0, t1) in zip(merge, MERGE):
                        flat = m_.rearrange("p t g h d -> p (t g h) d")[:, :, 0:HD]
                        c.step(dve, V.tensor_tensor(flat, flat, small[0][:, t0:t1].rearrange("p t g h -> p (t g h)").unsqueeze(2)
                                                    .to_broadcast([P, (t1 - t0) * GROUPS * HEADS, HD]), ALU.mult))
                        rows4 = attn_rows[:, t0:t1, :].rearrange("p t (h d) -> p t h d", h=HEADS)
                        c.step(dve, V.tensor_tensor(rows4, m_[:, :, 0, :, 0:HD], m_[:, :, 1, :, 0:HD], ALU.add))
                        c.step(dve, V.tensor_tensor(rows4, rows4, m_[:, :, 2, :, 0:HD], ALU.add))
                    dve.sem_inc(s_mrg, 1)
                    for t in range(NT):
                        dve.wait_ge(s_atp, t + 1)
                        r = rows_of(t)
                        V.tensor_copy(attn_t[:, :, t * P:t * P + r], bank[t % 2][:, 0:2 * P].rearrange("p (c n) -> p c n", c=2)[:, :, 0:r]).then_inc(s_ate, 1)

                @block.scalar
                def _(act):
                    A = nc.scalar
                    done = [0]

                    def finish(step):
                        for u in range(done[0], done[0] + FILL[step]):
                            act.wait_ge(s_gu, u + 1)
                            if u >= GB:
                                act.wait_ge(s_gst[u % GB], 16 * (u // GB))
                            A.activation(g_sb[:, u % GB, :], bank[4 + u % 4][:, 0:CW], ACT.Sigmoid,
                                         bias=prm_t[:, 64 + u // 3:65 + u // 3]).then_inc(s_gc, 1)
                            act.wait_ge(s_gc, u + 1)
                            act.dma_start(scratch["gates"][u // 3, :, u % 3 * CW:(u % 3 + 1) * CW], g_sb[:, u % GB, :]).then_inc(s_gst[u % GB], 16)
                            b = u // 6 + 2
                            if u % 6 == 5 and b < 8:
                                act.dma_start(ring[:, b % 2, :].rearrange("p (k c) -> p k c", k=KT),
                                              I["w_mgate"][0][:, b * WB:(b + 1) * WB].rearrange("(k p) c -> p k c", p=P)).then_inc(s_gw[b % 2], 16)
                        done[0] += FILL[step]

                    finish("start")
                    finish("params")
                    act.wait_ge(s_a1, 1)
                    A.activation(sm[:, 2, :], pc[:, 32:48], ACT.Exp).then_inc(s_a2, 1)
                    act.wait_ge(s_a3, 1)
                    A.activation(sm[:, 5, :], sm[:, 3, :], ACT.Exp).then_inc(s_a4, 1)
                    A.activation(sm[:, 6, :], sm[:, 3, :], ACT.Exp, scale=float(L)).then_inc(s_a4, 1)
                    act.wait_ge(s_a3, 2)
                    A.activation(sm[:, 8, :], sm[:, 4, :], ACT.Sin).then_inc(s_a5, 1)
                    A.activation(sm[:, 7, :], sm[:, 9, :], ACT.Sin).then_inc(s_a5, 1)
                    finish("c_h0")
                    for g in range(GROUPS):
                        wd = DK[g] + NS
                        finish(f"scores{g}")
                        finish(f"turn_scores{g}")
                        act.wait_ge(s_nx, g + 1)
                        A.activation(p2[:, 0:wd], s2[:, 0:wd], ACT.Exp, bias=d_sb[:, HD:HD + 1], scale=1.0,
                                     accum_out=d_sb[:, HD + 1:HD + 2]).then_inc(s_pe, 1)
                        finish(f"turn_probs{g}")
                        finish(f"values{g}")
                        act.wait_ge(s_op, g + 1)
                        A.activation(o2[:, :], bank[2][0:HD, 0:P], ACT.Copy).then_inc(s_oa, 1)
                        finish(f"rows{g}")
                        finish(f"next{g}")
                    finish("merge")
                    act.wait_ge(s_dif, 1)
                    A.activation(small[1][:, :, :, :], small[0][:, :, :, :], ACT.Exp, scale=-1.0).then_inc(s_ex, 1)
                    finish("merged")

        s_usz, s_usl, s_hc = sem("u_sample_cleared"), sem("u_sample_loaded"), sem("h0_in_place")
        s_dl, s_deye = sem("ssm_d_loaded"), sem("d_diagonal_ready")
        s_tz, s_g, s_ge, s_gd, s_toe = (sem("toeplitz_cleared"), sem("taps_in_psum"), sem("taps_copied"), sem("taps_ready"),
                                        sem("toeplitz_loaded"))
        s_ut, s_ue, s_ust = sem("u_t_in_psum"), sem("u_t_copied"), sem("u_sample_t_in_psum")
        s_wt, s_we, s_v, s_ve = sem("inject_t_in_psum"), sem("inject_copied"), sem("injected_in_psum"), sem("injected_copied")
        s_x, s_y, s_ye, s_ys, s_yse = (sem("states_ready"), sem("y_in_psum"), sem("y_activated"), sem("y_sample_in_psum"),
                                       sem("y_sample_activated"))
        s_yt, s_yte = sem("y_t_in_psum"), sem("y_t_copied")
        s_fin, s_fx, s_fxe, s_fo = sem("final_states_ready"), sem("final_states_in_psum"), sem("final_states_copied"), sem("states_stored")
        s_wg, s_gl, s_gs, s_gle = sem("w_glu_loaded"), sem("glu_in_psum"), sem("glu_sigmoid"), sem("glu_done")
        s_dve4 = sem("dve_chain4")

        with ExitStack() as st:
            u_t = sb("u_t", [P, SSM_G, NCH + 2 * DEC_B], stack=st)
            w_sb = sb("w_sb", [P, 2, 2, P], stack=st)
            vs = sb("v_sample", [P, 2, SP2, DEC_B], stack=st)
            fs = sb("f_sample", [P, 2, DEC_B, SP2], stack=st)
            f_out = sb("f_out", [P, 4, P], stack=st)
            d_row = w_sb[0:SSM_C].rearrange("p a i c -> p (a i c)")
            d_eye = f_out[0:SSM_C].rearrange("p i c -> p (i c)").rearrange("p (g c) -> p g c", g=SSM_G)
            sig = t_im.rearrange("p n c -> p (n c)")

            with nc.Block() as block:
                @block.sync
                def _(sp):
                    sp.dma_start(d_row, I["ssm_d"].to_broadcast([SSM_C, SSM_W])).then_inc(s_dl, 16)
                    sp.wait_ge(s_usz, 1)
                    for t in range(DEC_T):
                        src = scratch["u_new"].rearrange("(b t) (g c) -> t b g c", t=DEC_T, c=SSM_C)[t]
                        sp.dma_start(us[0:8, :, DEC_T + t, :], src).then_inc(s_usl, 16)
                        sp.dma_start(us[8:16, :, t, :], src).then_inc(s_usl, 16)
                    sp.wait_ge(s_gd, 1)
                    sp.wait_ge(s_tz, 1)
                    for j in range(L):
                        sp.dma_start(toe[SSM_C * j:SSM_C * (j + 1), :, SSM_C * j:P], g_all[:, :, 0:P - SSM_C * j]).then_inc(s_toe, 16)
                    sp.wait_ge(s_v, SP2)
                    sp.dma_start(ring[:, 3, :].rearrange("p (k c) -> p k c", k=4),
                                 I["w_glu"][0].rearrange("(k p) c -> p k c", p=P)).then_inc(s_wg, 16)
                    sp.wait_ge(s_fxe, 1)
                    for i, nm_ in enumerate(("p_re", "p_im")):
                        sp.dma_start(O[nm_][0, 0].rearrange("(n r) s -> n (r s)", r=2), f_out[0:SP2, i, :]).then_inc(s_fo, 16)
                    for i, nm_ in enumerate(("s_re", "s_im")):
                        sp.dma_start(O[nm_][0].rearrange("b (n r) s -> (b n) (r s)", r=2), f_out[:, 2 + i, :]).then_inc(s_fo, 16)
                    sp.wait_ge(s_fo, 64)

                @block.gpsimd
                def _(pool):
                    G = nc.gpsimd
                    G.memset(us.rearrange("p g j c -> p (g j c)"), 0.0).then_inc(s_usz, 1)
                    G.memset(toe.rearrange("p g c -> p (g c)"), 0.0).then_inc(s_tz, 1)

                @block.scalar
                def _(act):
                    A = nc.scalar
                    for i in range(8):
                        act.wait_ge(s_ut, i + 1)
                        A.activation(u_t[:, 4 * i:4 * i + 4, 0:NCH], bank[i % 2].rearrange("p (g c) -> p g c", g=4), ACT.Copy).then_inc(s_ue, 1)
                    act.wait_ge(s_ust, 1)
                    A.activation(u_t[:, :, NCH:NCH + 16], bank[2].rearrange("p (g c) -> p g c", c=16), ACT.Copy).then_inc(s_ue, 1)
                    for i in range(8):
                        act.wait_ge(s_g, i + 1)
                        A.activation(g_all.rearrange("p (n r) c -> p r n c", r=2)[:, i % 2, 4 * (i // 2):4 * (i // 2) + 4, :],
                                     bank[4 + i % 4][0:SSM_C].rearrange("p (n c) -> p n c", n=4), ACT.Copy).then_inc(s_ge, 1)
                    act.wait_ge(s_deye, 1)

                    def copy_w(n):
                        act.wait_ge(s_wt, n + 1)
                        if n >= 2:
                            act.wait_ge(s_v, n - 1)
                        A.activation(w_sb[:, n % 2, :, :], bank[4 + n % 2][:, 0:2 * P].rearrange("p (i c) -> p i c", i=2), ACT.Copy).then_inc(s_we, 1)

                    copy_w(0)
                    for n in range(SP2):
                        if n + 1 < SP2:
                            copy_w(n + 1)
                        act.wait_ge(s_v, n + 1)
                        src = bank[6 + n % 2]
                        src = src[:, 0:272].rearrange("p (i c) -> p i c", i=2)
                        A.activation(v_both[:, :, n, 1:1 + NCH], src[:, :, 0:NCH], ACT.Copy)
                        A.activation(vs[:, :, n, :], src[:, :, NCH:136], ACT.Copy).then_inc(s_ve, 1)
                    act.wait_ge(s_ue, 9)
                    for q in range(4):
                        act.wait_ge(s_y, q + 1)
                        for r in range(2):
                            m = A.activation(y_rows[:, :, 4 * q:4 * q + 4, r, :].rearrange("p i n c -> p n i c"),
                                             bank[2 * (q % 2) + r].rearrange("p (n i c) -> p n i c", n=4, i=L), ACT.Gelu_apprx_tanh)
                        m.then_inc(s_ye, 1)
                        act.wait_ge(s_ys, q + 1)
                        for r in range(2):
                            m = A.activation(ys[:, :, 4 * q:4 * q + 4, r, :].rearrange("p i n c -> p n i c"),
                                             bank[4 + r][0:DEC_B].rearrange("p (n i c) -> p n i c", n=4, i=L)[:, :, 0:DEC_T], ACT.Gelu_apprx_tanh)
                        m.then_inc(s_yse, 1)
                    for i in range(12):
                        act.wait_ge(s_gl, i + 1)
                        if i >= 2:
                            act.wait_ge(s_gle, i - 1)
                        A.activation(sig[:, (i % 2) * CW:(i % 2 + 1) * CW], bank[i % 2][:, 0:CW], ACT.Sigmoid).then_inc(s_gs, 1)

                @block.tensor
                def _(pe):
                    T_ = nc.tensor
                    for i in range(8):
                        if i >= 2:
                            pe.wait_ge(s_ue, i - 1)
                        for j in range(4):
                            m = T_.transpose(bank[i % 2][:, j * P:(j + 1) * P],
                                             u_rows[:, 4 * i + j, :, :].rearrange("p j c -> p (j c)"), ident[:, :])
                        m.then_inc(s_ut, 1)
                    pe.wait_ge(s_usl, 16 * 2 * DEC_T)
                    for g in range(SSM_G):
                        m = T_.transpose(bank[2][:, 16 * g:16 * g + 16], us[:, g, :, :].rearrange("p j c -> p (j c)"), ident[0:16, 0:16])
                    m.then_inc(s_ust, 1)
                    for i in range(8):
                        r, lo = i % 2, 64 * (i % 2)
                        if i >= 4:
                            pe.wait_ge(s_ge, i - 3)
                        for j in range(4):
                            n = 4 * (i // 2) + j
                            o = bank[4 + i % 4][0:SSM_C, j * P:(j + 1) * P]
                            for a, c0, c1 in ((0, cc[:, 0], ca_re), (1, cc[:, 1], ca_im)):
                                lhs = bb[lo:lo + 64, a, n, :]
                                T_.matmul(o[:, 0:SSM_C], lhs, c0[lo:lo + 64, n, :], start=(a == 0 and True), stop=(a == 1), skip_group_check=True)
                                m = T_.matmul(o[:, SSM_C:P], lhs, c1[lo:lo + 64, n, 0:L - 1, :].rearrange("p i c -> p (i c)"),
                                              start=False, stop=(a == 1), skip_group_check=True)
                        m.then_inc(s_g, 1)
                    pe.wait_ge(s_ge, 8)
                    pe.wait_ge(s_ue, 9)

                    def turn(n):
                        if n >= 2:
                            pe.wait_ge(s_we, n - 1)
                        for i, b_ in enumerate((ba_re, ba_im)):
                            m = T_.transpose(bank[4 + n % 2][:, i * P:(i + 1) * P], b_[:, n, :, :].rearrange("p j c -> p (j c)"), ident[:, :])
                        m.then_inc(s_wt, 1)

                    turn(0)
                    for n in range(SP2):
                        if n + 1 < SP2:
                            turn(n + 1)
                        pe.wait_ge(s_we, n + 1)
                        if n >= 2:
                            pe.wait_ge(s_ve, n - 1)
                        for i in range(2):
                            for r in range(2):
                                m = T_.matmul(bank[6 + n % 2][64 * r:64 * r + 64, 136 * i:136 * i + 136],
                                              w_sb[:, n % 2, i, 64 * r:64 * r + 64], u_t[:, 2 * n + r, 0:136], start=True, stop=True)
                        m.then_inc(s_v, 1)
                    pe.wait_ge(s_toe, 16 * L)
                    pe.wait_ge(s_ve, SP2)

                    def turn_y(ct):
                        pe.wait_ge(s_ye, ct + 1)
                        for x in (2 * ct, 2 * ct + 1):
                            if x >= 2:
                                pe.wait_ge(s_yte, x - 1)
                            for j in range(4):
                                m = T_.transpose(bank[6 + x % 2][:, j * P:(j + 1) * P],
                                                 y_rows[:, 4 * (x % 2) + j, 4 * ct:4 * ct + 4].rearrange("p n r c -> p (n r c)"), ident[:, :])
                            m.then_inc(s_yt, 1)

                    for q in range(4):
                        pe.wait_ge(s_x, q + 1)
                        if q >= 2:
                            pe.wait_ge(s_ye, q - 1)
                        if q:
                            pe.wait_ge(s_yse, q)
                        for smp, width, rows_, cols, uc in ((0, NCH, slice(0, P), slice(0, NCH), slice(0, NCH)),
                                                            (4, DEC_B, slice(0, DEC_B), slice(NCH + 1, NV), slice(136, 144))):
                            for j in range(4):
                                n = 4 * q + j
                                for r in range(2):
                                    lo = 64 * r
                                    i_n = L if smp == 0 else DEC_T
                                    o = bank[smp + (2 * (q % 2) if smp == 0 else 0) + r][rows_, j * P:j * P + i_n * SSM_C]
                                    T_.matmul(o, v_re[lo:lo + 64, n, cols], ca_re[lo:lo + 64, n, 0:i_n].rearrange("p i c -> p (i c)"), start=True, stop=False)
                                    T_.matmul(o, v_im[lo:lo + 64, n, cols], ca_im[lo:lo + 64, n, 0:i_n].rearrange("p i c -> p (i c)"), start=False, stop=False)
                                    m = T_.matmul(o, u_t[:, 2 * n + r, uc], toe[:, 2 * n + r, 0:i_n * SSM_C], start=False, stop=True)
                            m.then_inc(s_y if smp == 0 else s_ys, 1)
                        if q:
                            turn_y(q - 1)
                    turn_y(3)
                    pe.wait_ge(s_yse, 4)
                    for ct in range(4):
                        for i in range(DEC_T):
                            m = T_.transpose(bank[2][:, (ct * DEC_T + i) * 8:(ct * DEC_T + i) * 8 + 8],
                                             ys[:, i, 4 * ct:4 * ct + 4].rearrange("p n r c -> p (n r c)"), ident[0:8, 0:8])
                    m.then_inc(s_yt, 1)
                    pe.wait_ge(s_fin, 1)
                    for i, v_ in enumerate((v_re, v_im)):
                        T_.transpose(bank[3][0:SP2, i * P:(i + 1) * P], v_[:, :, NCH], ident[:, :])
                    for i in range(2):
                        m = T_.transpose(bank[3][:, (2 + i) * P:(3 + i) * P], fs[:, i, :, :].rearrange("p b n -> p (b n)"), ident[:, :])
                    m.then_inc(s_fx, 1)
                    pe.wait_ge(s_wg, 16)
                    pe.wait_ge(s_yte, 9)
                    wg = ring[:, 3, :].rearrange("p (k c) -> p k c", k=4)
                    for i in range(12):
                        ct, n = i // CH, i % CH
                        if i >= 2:
                            pe.wait_ge(s_gs, i - 1)
                        for k in range(4):
                            m = T_.matmul(bank[i % 2][:, 0:CW], wg[:, k, ct * P:(ct + 1) * P], y_t[:, k, n * CW:(n + 1) * CW],
                                          start=(k == 0), stop=(k == 3))
                        m.then_inc(s_gl, 1)

                @block.vector
                def _(dve):
                    V = nc.vector
                    c = Counted(s_dve4)

                    def tt(out, a, b, op):
                        c.step(dve, V.tensor_tensor(out, a, b, op))

                    def cmul(o_re, o_im, a_re_, a_im_, b_re_, b_im_, tmp):
                        tt(o_re, a_re_, b_re_, ALU.mult)
                        tt(tmp, a_im_, b_im_, ALU.mult)
                        tt(o_re, o_re, tmp, ALU.subtract)
                        tt(o_im, a_re_, b_im_, ALU.mult)
                        tt(tmp, a_im_, b_re_, ALU.mult)
                        tt(o_im, o_im, tmp, ALU.add)

                    dve.wait_ge(s_ust, 1)
                    c.step(dve, V.memset(v_re[:, :, 0], 0.0))
                    c.step(dve, V.memset(v_im[:, :, 0], 0.0))
                    c.step(dve, V.tensor_copy(v_re[:, :, NCH + 1:NV], h0[:, 0]))
                    c.step(dve, V.tensor_copy(v_im[:, :, NCH + 1:NV], h0[:, 1]))
                    dve.wait_ge(s_dl, 16)
                    V.tensor_tensor(d_eye, d_row.rearrange("p (g c) -> p g c", g=SSM_G),
                                    ident[0:SSM_C, 0:SSM_C].unsqueeze(1).to_broadcast([SSM_C, SSM_G, SSM_C]), ALU.mult).then_inc(s_deye, 1)
                    dve.wait_ge(s_deye, 1)
                    dve.wait_ge(s_ge, 8)
                    V.tensor_tensor(g_all[:, :, 0:SSM_C], g_all[:, :, 0:SSM_C], d_eye, ALU.add).then_inc(s_gd, 1)
                    dve.wait_ge(s_gd, 1)
                    dve.wait_ge(s_toe, 16 * L)
                    for q in range(4):
                        dve.wait_ge(s_ve, 4 * (q + 1))
                        n4 = slice(4 * q, 4 * q + 4)
                        xr_, xi_ = v_re[:, n4, 1:1 + NCH], v_im[:, n4, 1:1 + NCH]
                        er_, ei_, tr_, ti_ = e_re[:, n4], e_im[:, n4], t_re[:, n4], t_im[:, n4]
                        V.tensor_tensor(tr_, xi_, ei_, ALU.mult)
                        tt(ti_, xr_, ei_, ALU.mult)
                        V.tensor_tensor(xr_, xr_, er_, ALU.mult)
                        tt(xi_, xi_, er_, ALU.mult)
                        V.tensor_tensor(xr_, xr_, tr_, ALU.add)
                        tt(xi_, xi_, ti_, ALU.subtract)
                        for n in range(4 * q, 4 * q + 4):
                            rho = sm[:, 6, n:n + 1].to_broadcast([P, NCH])
                            V.tensor_tensor_scan(t_re[:, n, :], rho, v_re[:, n, 1:1 + NCH], 0.0, ALU.mult, ALU.add)
                            m = V.tensor_tensor_scan(t_im[:, n, :], rho, v_im[:, n, 1:1 + NCH], 0.0, ALU.mult, ALU.add)
                        c.step(dve, m)
                        V.tensor_tensor(xr_, tr_, er_, ALU.mult)
                        tt(xi_, tr_, ei_, ALU.mult)
                        V.tensor_tensor(tr_, ti_, ei_, ALU.mult)
                        tt(ti_, ti_, er_, ALU.mult)
                        V.tensor_tensor(xr_, xr_, tr_, ALU.subtract)
                        tt(xi_, xi_, ti_, ALU.add)
                        dve.sem_inc(s_x, 1)
                    sh = [P, SP2, DEC_B]
                    a4r, a4i = (pw[:, i, DEC_T, :].unsqueeze(2).to_broadcast(sh) for i in range(2))
                    h0r, h0i = v_re[:, :, NCH + 1:NV], v_im[:, :, NCH + 1:NV]
                    fr_, fi_ = (fs[:, i].rearrange("p b n -> p n b") for i in range(2))
                    cmul(fr_, fi_, a4r, a4i, h0r, h0i, tp[:, 0:128].rearrange("p (n b) -> p n b", n=SP2))
                    tt(fr_, fr_, vs[:, 0], ALU.add)
                    tt(fi_, fi_, vs[:, 1], ALU.add)
                    dve.sem_inc(s_fin, 1)
                    for x in range(8):
                        ct, i0 = x // 2, 4 * (x % 2)
                        dve.wait_ge(s_yt, x + 1)
                        V.tensor_copy(y_t[:, ct, 0:SEQ].rearrange("p (c i) -> p i c", i=L)[:, i0:i0 + 4, :],
                                      bank[6 + x % 2].rearrange("p (i c) -> p i c", i=4)).then_inc(s_yte, 1)
                    dve.wait_ge(s_yt, 9)
                    for ct in range(4):
                        m = V.tensor_copy(y_t[:, ct, SEQ:N].rearrange("p (b i) -> p i b", i=DEC_T),
                                          bank[2][:, ct * 32:(ct + 1) * 32].rearrange("p (i b) -> p i b", i=DEC_T))
                    m.then_inc(s_yte, 1)
                    dve.wait_ge(s_fx, 1)
                    V.tensor_copy(f_out[0:SP2, 0:2, :], bank[3][0:SP2, 0:2 * P].rearrange("p (i c) -> p i c", i=2))
                    V.tensor_copy(f_out[:, 2:4, :], bank[3][:, 2 * P:4 * P].rearrange("p (i c) -> p i c", i=2)).then_inc(s_fxe, 1)
                    for i in range(12):
                        ct, n = i // CH, i % CH
                        dve.wait_ge(s_gs, i + 1)
                        V.tensor_tensor(y2_t[:, ct, n * CW:(n + 1) * CW], y_t[:, ct, n * CW:(n + 1) * CW],
                                        sig[:, (i % 2) * CW:(i % 2 + 1) * CW], ALU.mult).then_inc(s_gle, 1)
        st34.close()

        nc.clear_and_free_semaphores(front_sems)
        nc.all_engine_barrier()
        front_sems = None
        VEC = ("gate1", "gain2", "shift2", "gate2")
        u_flat = u_rows[:, :, :, :].rearrange("p g j c -> p (g j c)")
        row_p = {v: u_flat[:, i * D:(i + 1) * D] for i, v in enumerate(VEC)}
        row_s = {v: big[0:NS, 2112 + i * D:2112 + (i + 1) * D] for i, v in enumerate(VEC)}
        merged_t = big[:, 10560:19008].rearrange("p (k n) -> p k n", k=KT)
        x2 = h_t[:, 0:TT * D].rearrange("p (t d) -> p t d", t=TT)
        x2_s = big[0:NS, 6336:6336 + D]
        h2_row = [big[:, 7360 + i * D:7360 + (i + 1) * D] for i in range(2)]
        sq5 = big[:, 9408:9408 + D]
        logits = sb("logits", [P, NT, NG + NE])
        row_bias = sb("router_bias", [P, NG + NE])

        def x2_of(t):
            return x2[:, t, :] if t < TT else x2_s

        GL = 3
        s_w5 = [sem(f"weights5_{i}_loaded") for i in range(RING)]
        s_br, s_rt, s_rb, s_xr5 = sem("branch_w_loaded"), sem("router_w_loaded"), sem("router_b_loaded"), sem("x_rows_again")
        s_gl5 = [sem(f"gates{i}_loaded") for i in range(GL)]
        s_exp, s_vt, s_vc, s_vd = sem("vectors_expanded"), sem("vectors_in_psum"), sem("vectors_copied_act"), sem("vectors_copied_dve")
        s_mu, s_md = sem("merge_unit_in_psum"), sem("merge_unit_done")
        s_op5, s_x2, s_sq5, s_m5, s_rt5, s_h2 = (sem("out_in_psum"), sem("x2_ready"), sem("x2_squares"), sem("x2_mean_square"),
                                                 sem("x2_root"), sem("h2_ready"))
        s_ht5, s_hc5, s_lg, s_lgc, s_h2s = (sem("h2_t_in_psum"), sem("h2_t_copied"), sem("logits_in_psum"), sem("logits_ready"),
                                            [sem(f"h2_rows_stored{i}") for i in range(2)])
        s_dve5 = sem("dve_chain5")

        with ExitStack() as st:
            w_bs = sb("w_br_ssm", [P, 4, D], stack=st)
            w_ba = sb("w_br_attn", [P, 2, D], stack=st)
            sg = sb("gate_units5", [P, GL, 2, CW], stack=st)
            w_r = w_bs[:, 0:1, 0:KT * 36].rearrange("p a (k e) -> p (a k) e", k=KT)
            h2_t = w_ba[:, 0, :].rearrange("p (k n) -> p k n", k=KT)
            ex = big[:, 10560:10560 + 4 * KT * NS].rearrange("p (v k n) -> p v k n", v=4, k=KT)
            ss5 = sb("ss5", [P, NT], stack=st)
            w_o = I["w_out"][0]

            with nc.Block() as block:
                @block.sync
                def _(sp):
                    sp.dma_start(w_bs[:, :, :], I["w_br_ssm"][0].rearrange("(k p) c -> p k c", p=P)).then_inc(s_br, 16)
                    sp.dma_start(w_ba[:, :, :], I["w_br_attn"][0].rearrange("(k p) c -> p k c", p=P)).then_inc(s_br, 16)
                    for u in range(8 * CH):
                        if u >= GL:
                            sp.wait_ge(s_md, u - GL + 1)
                        for i in range(2):
                            sp.dma_start(sg[:, u % GL, i, :], scratch["gates"][8 * i + u // CH, :, u % CH * CW:(u % CH + 1) * CW]).then_inc(s_gl5[u % GL], 16)
                        if 3 <= u < 7:
                            sp.dma_start(ring[:, u - 3, :].rearrange("p (k c) -> p k c", k=KT),
                                         w_o[:, (u - 3) * WB:(u - 2) * WB].rearrange("(k p) c -> p k c", p=P)).then_inc(s_w5[u - 3], 16)
                        if 7 <= u < 7 + TT:
                            sp.dma_start(x2[:, u - 7, :], I["x_prompt"][0, (u - 7) * P:(u - 6) * P, :]).then_inc(s_xr5, 16)
                    sp.wait_ge(s_md, 8 * CH)
                    sp.dma_start(x2_s, I["x_sample"].rearrange("b t d -> (b t) d")).then_inc(s_xr5, 16)
                    sp.dma_start(w_r[:, :, 0:NG], I["w_router_grp"][0].rearrange("(k p) e -> p k e", p=P)).then_inc(s_rt, 16)
                    sp.dma_start(w_r[:, :, NG:NG + NE], I["w_router_exp"][0].rearrange("(k p) e -> p k e", p=P)).then_inc(s_rt, 16)
                    sp.dma_start(row_bias[:, 0:NG], I["b_router_grp"].to_broadcast([P, NG])).then_inc(s_rb, 16)
                    sp.dma_start(row_bias[:, NG:NG + NE], I["b_router_exp"].to_broadcast([P, NE])).then_inc(s_rb, 16)
                    for t in range(NT):
                        sp.wait_ge(s_h2, t + 1)
                        r = rows_of(t)
                        sp.dma_start(scratch["h2_rows"][t * P:t * P + r, :], h2_row[t % 2][0:r, :]).then_inc(s_h2s[t % 2], 16)
                    sp.wait_ge(s_h2s[0], 16 * 5)
                    sp.wait_ge(s_h2s[1], 16 * 4)

                @block.tensor
                def _(pe):
                    T_ = nc.tensor
                    pe.wait_ge(s_exp, 1)
                    for v, src in enumerate((mod_t[:, 16:24, :], gain1[:, :, :], mod_t[:, 24:32, :], mod_t[:, 40:48, :])):
                        if v >= 2:
                            pe.wait_ge(s_vc, v - 1)
                            pe.wait_ge(s_vd, v - 1)
                        b0 = 4 * (v % 2)
                        for k in range(KT):
                            T_.transpose(bank[b0 + k // 4][:, (k % 4) * P:(k % 4 + 1) * P], src[:, k, 0:1].to_broadcast([P, P]), ident[:, :])
                            m = T_.transpose(bank[b0 + 2 + k // 4][0:NS, (k % 4) * P:(k % 4 + 1) * P], ex[:, v, k, :], ident[:, :])
                        m.then_inc(s_vt, 1)
                    pe.wait_ge(s_vc, 4)
                    pe.wait_ge(s_vd, 4)
                    pe.wait_ge(s_br, 32)
                    for m_ in range(8):
                        for j in range(CH):
                            u = m_ * CH + j
                            tok = slice(j * CW, (j + 1) * CW)
                            b0 = 4 * (u % 2)
                            if u >= 2:
                                pe.wait_ge(s_md, u - 1)
                            for k in range(4):
                                T_.matmul(bank[b0 + 2][:, 0:CW], w_bs[:, k, m_ * P:(m_ + 1) * P], y2_t[:, k, tok], start=(k == 0), stop=(k == 3))
                            for k in range(2):
                                m = T_.matmul(bank[b0 + 3][:, 0:CW], w_ba[:, k, m_ * P:(m_ + 1) * P], attn_t[:, k, tok], start=(k == 0), stop=(k == 1))
                            m.then_inc(s_mu, 1)
                    pe.wait_ge(s_md, 8 * CH)
                    for n in range(4):
                        pe.wait_ge(s_w5[n], 16)

                    def out_tile(t):
                        r = rows_of(t)
                        if t >= 2:
                            pe.wait_ge(s_x2, t - 1)
                        for b in range(4):
                            w = ring[:, b, :].rearrange("p (k c) -> p k c", k=KT)
                            for k in range(KT):
                                m = T_.matmul(bank[2 * (t % 2) + b // 2][0:r, (b % 2) * WB:(b % 2 + 1) * WB],
                                              merged_t[:, k, t * P:t * P + r], w[:, k, :], start=(k == 0), stop=(k == KT - 1))
                        m.then_inc(s_op5, 1)

                    def turn_h2(t):
                        r = rows_of(t)
                        pe.wait_ge(s_h2, t + 1)
                        if t >= 1:
                            pe.wait_ge(s_hc5, t)
                        for k in range(KT):
                            m = T_.transpose(bank[4 + k // 4][:, (k % 4) * P:(k % 4) * P + r], h2_row[t % 2][0:r, k * P:(k + 1) * P], ident[0:r, 0:r])
                        m.then_inc(s_ht5, 1)

                    def route(t):
                        r = rows_of(t)
                        pe.wait_ge(s_hc5, t + 1)
                        if t == 0:
                            pe.wait_ge(s_rt, 32)
                        if t >= 2:
                            pe.wait_ge(s_lgc, t - 1)
                        for k in range(KT):
                            m = T_.matmul(bank[6 + t % 2][0:r, 0:NG + NE], h2_t[:, k, 0:r], w_r[:, k, :], start=(k == 0), stop=(k == KT - 1))
                        m.then_inc(s_lg, 1)

                    for t in range(NT + 2):
                        if t < NT:
                            out_tile(t)
                        if t >= 2:
                            route(t - 2)
                        if 1 <= t <= NT:
                            turn_h2(t - 1)

                @block.scalar
                def _(act):
                    A = nc.scalar
                    for v in range(4):
                        act.wait_ge(s_vt, v + 1)
                        b0 = 4 * (v % 2)
                        A.activation(row_p[VEC[v]].rearrange("p (b c) -> p b c", b=2), psum[:, b0:b0 + 2, :], ACT.Copy).then_inc(s_vc, 1)
                    for t in range(NT + 1):
                        if t < NT:
                            r = rows_of(t)
                            act.wait_ge(s_x2, t + 1)
                            if t:
                                act.wait_ge(s_sq5, t)
                            A.activation(sq5[0:r, :], x2_of(t)[0:r, :], ACT.Square, accum_out=ss5[0:r, t:t + 1]).then_inc(s_sq5, 1)
                            act.wait_ge(s_m5, t + 1)
                            A.activation(ss5[0:r, t:t + 1], ss5[0:r, t:t + 1], ACT.Sqrt).then_inc(s_rt5, 1)
                        if t >= 1:
                            r = rows_of(t - 1)
                            act.wait_ge(s_ht5, t)
                            if t >= 2:
                                act.wait_ge(s_lg, t - 1)
                            A.activation(h2_t.rearrange("p (b k) n -> p b k n", b=2)[:, :, :, 0:r],
                                         psum[:, 4:6, :].rearrange("p b (k n) -> p b k n", k=4)[:, :, :, 0:r], ACT.Copy).then_inc(s_hc5, 1)

                @block.vector
                def _(dve):
                    V = nc.vector
                    c = Counted(s_dve5)
                    c.step(dve, V.tensor_scalar(gain1[:, :, :], mod_t[:, 32:40, :], 1.0, None, ALU.add))
                    c.step(dve, V.tensor_tensor(gain1[:, :, :], gain1[:, :, :], prm_t[:, 56:64].unsqueeze(2).to_broadcast([P, KT, 9]), ALU.mult))
                    for v, src in enumerate((mod_t[:, 16:24, :], gain1[:, :, :], mod_t[:, 24:32, :], mod_t[:, 40:48, :])):
                        m = V.tensor_copy(ex[:, v].rearrange("p k (b t) -> p k b t", t=DEC_T),
                                          src[:, :, 1:9].unsqueeze(3).to_broadcast([P, KT, DEC_B, DEC_T]))
                    m.then_inc(s_exp, 1)
                    for v in range(4):
                        dve.wait_ge(s_vt, v + 1)
                        V.tensor_copy(row_s[VEC[v]].rearrange("p (b c) -> p b c", b=2), psum[0:NS, 4 * (v % 2) + 2:4 * (v % 2) + 4, :]).then_inc(s_vd, 1)
                    c.step(dve, V.memset(logits[:, :, :], 0.0))
                    for u in range(8 * CH):
                        m_, j = u // CH, u % CH
                        tok = slice(j * CW, (j + 1) * CW)
                        b0 = 4 * (u % 2)
                        dve.wait_ge(s_mu, u + 1)
                        dve.wait_ge(s_gl5[u % GL], 32 * (u // GL + 1))
                        V.tensor_tensor(sg[:, u % GL, 0, :], sg[:, u % GL, 0, :], bank[b0 + 2][:, 0:CW], ALU.mult)
                        c.step(dve, V.tensor_tensor(sg[:, u % GL, 1, :], sg[:, u % GL, 1, :], bank[b0 + 3][:, 0:CW], ALU.mult))
                        V.tensor_tensor(merged_t[:, m_, tok], sg[:, u % GL, 0, :], sg[:, u % GL, 1, :], ALU.add).then_inc(s_md, 1)
                    for t in range(NT + 2):
                        if t < NT:
                            r = rows_of(t)
                            rows_ = row_p if t < TT else row_s
                            dve.wait_ge(s_op5, t + 1)
                            if t == 0:
                                dve.wait_ge(s_xr5, 16 * NT)
                            h2 = h2_row[t % 2][0:r, :]
                            if t >= 2:
                                dve.wait_ge(s_h2s[t % 2], 16 * (t // 2))
                                dve.wait_ge(s_ht5, t - 1)
                            c.step(dve, V.tensor_tensor(h2.rearrange("p (b c) -> p b c", b=2),
                                                        psum[0:r, 2 * (t % 2):2 * (t % 2) + 2, :],
                                                        rows_["gate1"][0:r, :].rearrange("p (b c) -> p b c", b=2), ALU.mult))
                            V.tensor_tensor(x2_of(t)[0:r, :], x2_of(t)[0:r, :], h2, ALU.add).then_inc(s_x2, 1)
                            dve.wait_ge(s_sq5, t + 1)
                            V.tensor_scalar(ss5[0:r, t:t + 1], ss5[0:r, t:t + 1], 1.0 / D, EPS, ALU.mult, ALU.add).then_inc(s_m5, 1)
                            dve.wait_ge(s_rt5, t + 1)
                            c.step(dve, V.reciprocal(ss5[0:r, t:t + 1], ss5[0:r, t:t + 1]))
                            c.step(dve, V.scalar_tensor_tensor(out=h2, in0=x2_of(t)[0:r, :], scalar=ss5[0:r, t:t + 1], in1=rows_["gain2"][0:r, :],
                                                               op0=ALU.mult, op1=ALU.mult))
                            V.tensor_tensor(h2, h2, rows_["shift2"][0:r, :], ALU.add).then_inc(s_h2, 1)
                        if t >= 2:
                            r = rows_of(t - 2)
                            dve.wait_ge(s_lg, t - 1)
                            if t == 2:
                                dve.wait_ge(s_rb, 32)
                            V.tensor_tensor(logits[0:r, t - 2, :], bank[6 + t % 2][0:r, 0:NG + NE], row_bias[0:r, :], ALU.add).then_inc(s_lgc, 1)

        slot_i = sb("slot_i", [P, 2, NT], I32)
        w_top = sb("w_top", [P, 2, NT])
        tok_i = sb("token_of_slot", [P, NBLK], I32)
        blk_i = sb("expert_of_block", [1, NBLK + 1], I32)
        s_io6, s_tri, s_r1, s_r2, s_r3, s_r4 = (sem("iotas_ready"), sem("triangle_ready"), sem("group_shifted"), sem("group_exp"),
                                                sem("expert_shifted"), sem("expert_exp"))
        s_cnt, s_rank, s_oh, s_tp = (sem("members_ready"), sem("ranks_in_psum"), sem("one_hots_ready"),
                                     sem("slot_tokens_in_psum"))
        s_dve6, s_pool6 = sem("dve_chain6"), sem("pool_chain6")
        s_wgu, s_wdn = [sem(f"w_gate_up{i}_loaded") for i in range(2)], [sem(f"w_down{i}_loaded") for i in range(2)]
        s_gup, s_dn, s_blk = sem("gate_up_in_psum"), sem("down_in_psum"), sem("blocks_ready")
        ring_all = ring[:, :, :].rearrange("p s c -> p (s c)")

        w_gu = [ring_all[:, 4096 * i:4096 * (i + 1)].rearrange("p (k c) -> p k c", k=KT) for i in range(2)]
        w_dn = [big[:, 7360 + 2048 * i:9408 + 2048 * i].rearrange("p (k c) -> p k c", k=2) for i in range(2)]

        def load_weights(sp):
            def load(b, i, guard):
                e = sp.value_load(blk_i[0:1, bass.ds(b, 1)], min_val=0, max_val=NE - 1)
                if guard is not None:
                    sp.wait_ge(s_gup, b - 1)
                for a, name in enumerate(("w_exp_gate", "w_exp_up")):
                    sp.dma_start(w_gu[i][:, :, a * FF:(a + 1) * FF],
                                 I[name][0][bass.ds(e, 1)].rearrange("o (k p) f -> p (o k) f", p=P)).then_inc(s_wgu[i], 16)
                if guard is not None:
                    sp.wait_ge(s_dn, b - 1)
                sp.dma_start(w_dn[i], I["w_exp_down"][0][bass.ds(e, 1)].rearrange("o (k p) f -> p (o k) f", p=P)).then_inc(s_wdn[i], 16)
            return load

        with ExitStack() as st:
            seq = sb("iota_f", [P, P], stack=st)
            seq_i = sb("iota_i", [P, P], I32, stack=st)
            place_i = sb("place_i", [P, 2, 2 * NT], I32, stack=st)
            ids_i = sb("ids_i", [P, NT], I32, stack=st)
            ids = sb("ids", [P, NT], stack=st)
            tri = sb("tri", [P, P], stack=st)
            ones = sb("ones", [P, P], stack=st)
            R = big[:, 11456:19584]
            at = [0]

            def take(*shape):
                n = int(np.prod(shape))
                v = R[:, at[0]:at[0] + n]
                at[0] += n
                if len(shape) == 2:
                    v = v.rearrange("p (a b) -> p a b", a=shape[0])
                if len(shape) == 3:
                    v = v.rearrange("p (a b c) -> p a b c", a=shape[0], b=shape[1])
                return v

            gmax, gsum, vmin, lmax, lsum, p1, p2_, s12 = (take(NT) for _ in range(8))
            eg, eq4, ohg = (take(NT, NG) for _ in range(3))
            lsel, e8, eq8 = (take(NT, EPG) for _ in range(3))
            oh = [take(NT, EPG) for _ in range(2)]
            prod = take(NT, NG, EPG)
            mem = [take(NT, NG, EPG) for _ in range(2)]
            both, before, pos = take(NT, NE), take(NT, NE), take(NT, NE)
            slot_f = take(2, NT)
            cnt, blocks, incl, start = (take(NE) for _ in range(4))
            cmp_ = take(NBLK + 1, NE)
            blk_f = take(NBLK + 1)
            place = take(2, 2 * NT)
            at_place, in_block = take(2 * NT, P), take(2 * NT, NBLK)

            with nc.Block() as block:
                @block.gpsimd
                def _(pool):
                    G = nc.gpsimd
                    c = Counted(s_pool6)
                    G.iota(seq_i[:, :], pattern=[[1, P]], base=0, channel_multiplier=0).then_inc(s_io6, 1)
                    G.iota(ids_i[:, :], pattern=[[P, NT]], base=0, channel_multiplier=1).then_inc(s_io6, 1)
                    c.step(pool, G.memset(tri[:, :], 1.0))
                    G.affine_select(out=tri[:, :], in_=tri[:, :], compare_op=ALU.is_gt, fill=0.0, base=0,
                                    pattern=[[1, P]], channel_multiplier=-1).then_inc(s_tri, 1)

                @block.sync
                def _(sp):
                    sp.wait_ge(s_blk, 1)
                    for b in range(2):
                        load_weights(sp)(b, b, None)

                @block.tensor
                def _(pe):
                    pe.wait_ge(s_cnt, 1)
                    pe.wait_ge(s_tri, 1)
                    f = "p t e -> p (t e)"
                    nc.tensor.matmul(bank[0][:, 0:NT * NE], tri[:, :], both.rearrange(f), start=True, stop=False)
                    nc.tensor.matmul(bank[0][:, 0:NT * NE], ones[:, :], before.rearrange(f), start=False, stop=True)
                    nc.tensor.matmul(bank[1][:, 0:NE], ones[:, :], both[:, TT, :], start=True, stop=False)
                    nc.tensor.matmul(bank[1][:, 0:NE], ones[:, :], before[:, TT, :], start=False, stop=True).then_inc(s_rank, 1)
                    pe.wait_ge(s_oh, 1)
                    for x in range(2 * NT):
                        m = nc.tensor.matmul(bank[2][:, 0:NBLK], at_place[:, x, :], in_block[:, x, :], start=(x == 0), stop=(x == 2 * NT - 1))
                    m.then_inc(s_tp, 1)

                @block.scalar
                def _(act):
                    act.wait_ge(s_r1, 1)
                    nc.scalar.activation(eg, eg, ACT.Exp).then_inc(s_r2, 1)
                    act.wait_ge(s_r3, 1)
                    nc.scalar.activation(e8, e8, ACT.Exp).then_inc(s_r4, 1)

                @block.vector
                def _(dve):
                    V = nc.vector
                    c = Counted(s_dve6)

                    def tt(out, a, b, op):
                        c.step(dve, V.tensor_tensor(out, a, b, op))

                    def red(out, in_, op):
                        c.step(dve, V.tensor_reduce(out, in_, AX.X, op))

                    def wide(v, n):
                        return v.unsqueeze(2).to_broadcast([P, NT, n])

                    c.step(dve, V.memset(ones[:, :], 1.0))
                    dve.wait_ge(s_io6, 2)
                    c.step(dve, V.tensor_copy(seq[:, :], seq_i[:, :]))
                    c.step(dve, V.tensor_copy(ids[:, :], ids_i[:, :]))
                    c.step(dve, V.memset(ids[NS:2 * NS, TT:NT], 0.0))
                    c.step(dve, V.memset(ids[2 * NS:P, TT:NT], 0.0))

                    def first_of(out, values, best, eq, n):
                        tt(eq, values, wide(best, n), ALU.is_equal)
                        c.step(dve, V.scalar_tensor_tensor(out=eq, in0=eq, scalar=-64.0, in1=seq[:, 0:n].unsqueeze(1).to_broadcast([P, NT, n]),
                                                           op0=ALU.mult, op1=ALU.add))
                        red(vmin, eq, ALU.min)
                        tt(out, eq, wide(vmin, n), ALU.is_equal)

                    lg, le = logits[:, :, 0:NG], logits[:, :, NG:NG + NE]
                    red(gmax, lg, ALU.max)
                    tt(eg, lg, wide(gmax, NG), ALU.subtract)
                    dve.sem_inc(s_r1, 1)
                    first_of(ohg, lg, gmax, eq4, NG)
                    tt(prod, le.rearrange("p t (g k) -> p t g k", g=NG), ohg.unsqueeze(3).to_broadcast([P, NT, NG, EPG]), ALU.mult)
                    red(lsel, prod.rearrange("p t g k -> p t k g"), ALU.add)
                    red(lmax, lsel, ALU.max)
                    tt(e8, lsel, wide(lmax, EPG), ALU.subtract)
                    dve.sem_inc(s_r3, 1)
                    dve.wait_ge(s_r2, 1)
                    red(gsum, eg, ALU.add)
                    c.step(dve, V.reciprocal(gsum, gsum))
                    dve.wait_ge(s_r4, 1)
                    red(lsum, e8, ALU.add)
                    c.step(dve, V.reciprocal(lsum, lsum))
                    tt(e8, e8, wide(lsum, EPG), ALU.mult)
                    red(p1, e8, ALU.max)
                    first_of(oh[0], e8, p1, eq8, EPG)
                    c.step(dve, V.scalar_tensor_tensor(out=e8, in0=oh[0], scalar=-4.0, in1=e8, op0=ALU.mult, op1=ALU.add))
                    red(p2_, e8, ALU.max)
                    first_of(oh[1], e8, p2_, eq8, EPG)
                    tt(s12, p1, p2_, ALU.add)
                    c.step(dve, V.reciprocal(s12, s12))
                    tt(s12, s12, gsum, ALU.mult)
                    tt(w_top[:, 0, :], p1, s12, ALU.mult)
                    tt(w_top[:, 1, :], p2_, s12, ALU.mult)
                    for k in range(2):
                        tt(mem[k], ohg.unsqueeze(3).to_broadcast([P, NT, NG, EPG]), oh[k].unsqueeze(2).to_broadcast([P, NT, NG, EPG]), ALU.mult)
                        c.step(dve, V.memset(mem[k][NS:2 * NS, TT], 0.0))
                        c.step(dve, V.memset(mem[k][2 * NS:P, TT], 0.0))
                    m1, m2 = (m.rearrange("p t g k -> p t (g k)") for m in mem)
                    tt(both, m1, m2, ALU.add)
                    c.step(dve, V.memset(before[:, 0, :], 0.0))
                    for t in range(1, NT):
                        tt(before[:, t, :], before[:, t - 1, :], both[:, t - 1, :], ALU.add)
                    dve.sem_inc(s_cnt, 1)
                    dve.wait_ge(s_rank, 1)
                    ci = cnt.bitcast(I32)
                    c.step(dve, V.tensor_scalar(ci, bank[1][:, 0:NE], 127.0, None, ALU.add))
                    c.step(dve, V.tensor_scalar(ci, ci, 7, None, ALU.logical_shift_right))
                    c.step(dve, V.tensor_copy(blocks, ci))
                    c.step(dve, V.tensor_tensor_scan(incl, ones[:, 0:NE], blocks, 0.0, ALU.mult, ALU.add))
                    tt(cmp_[0:1, 0:NBLK], incl[0:1, :].unsqueeze(1).to_broadcast([1, NBLK, NE]),
                       seq[0:1, 0:NBLK].unsqueeze(2).to_broadcast([1, NBLK, NE]), ALU.is_le)
                    red(blk_f[0:1, 0:NBLK], cmp_[0:1, 0:NBLK], ALU.add)
                    c.step(dve, V.tensor_scalar(blk_f[0:1, 0:NBLK], blk_f[0:1, 0:NBLK], float(NE - 1), None, ALU.min))
                    c.step(dve, V.tensor_scalar(blk_f[0:1, NBLK:NBLK + 1], incl[0:1, NE - 1:NE], -1.0, None, ALU.add))
                    c.step(dve, V.tensor_copy(blk_i[:, :], blk_f[0:1, :]))
                    c.step(dve, V.tensor_scalar(blk_i[:, NBLK:NBLK + 1], blk_i[:, NBLK:NBLK + 1], 1, None, ALU.logical_shift_right))
                    dve.sem_inc(s_blk, 1)
                    tt(start, incl, blocks, ALU.subtract)
                    c.step(dve, V.scalar_tensor_tensor(out=pos, in0=start.unsqueeze(1).to_broadcast([P, NT, NE]), scalar=float(P),
                                                       in1=bank[0][:, 0:NT * NE].rearrange("p (t e) -> p t e", t=NT), op0=ALU.mult, op1=ALU.add))
                    for k, m in enumerate((m1, m2)):
                        tt(before, m, pos, ALU.mult)
                        red(slot_f[:, k, :], before, ALU.add)
                    c.step(dve, V.tensor_copy(slot_i[:, :, :], slot_f))
                    slots = slot_i[:, :, :].rearrange("p k t -> p (k t)")
                    c.step(dve, V.tensor_scalar(place_i[:, 0, :], slots, 7, None, ALU.logical_shift_right))
                    c.step(dve, V.tensor_scalar(place_i[:, 1, :], slots, P - 1, None, ALU.bitwise_and))
                    c.step(dve, V.tensor_copy(place, place_i[:, :, :]))
                    sh = [P, 2 * NT, P]
                    tt(at_place, seq[:, :].unsqueeze(1).to_broadcast(sh), place[:, 1, :].unsqueeze(2).to_broadcast(sh), ALU.is_equal)
                    sh = [P, 2 * NT, NBLK]
                    tt(in_block, seq[:, 0:NBLK].unsqueeze(1).to_broadcast(sh), place[:, 0, :].unsqueeze(2).to_broadcast(sh), ALU.is_equal)
                    for k in range(2):
                        half = in_block[:, k * NT:(k + 1) * NT, :]
                        tt(half, half, ids[:, :].unsqueeze(2).to_broadcast([P, NT, NBLK]), ALU.mult)
                    dve.sem_inc(s_oh, 1)
                    dve.wait_ge(s_tp, 1)
                    c.step(dve, V.tensor_copy(tok_i[:, :], bank[2][:, 0:NBLK]))

        def loop_turns(eng):
            return eng.value_load(blk_i[0:1, NBLK:NBLK + 1], min_val=MIN_TURNS, max_val=NBLK // 2 - 1)

        s_xg = [sem(f"x_gathered{i}") for i in range(2)]
        s_ixs, s_yseen = sem("index_seen"), sem("stores_seen")
        s_yst = [sem(f"expert_rows{i}_stored") for i in range(2)]
        s_ix, s_tx, s_txc, s_sil, s_hid = (sem("index_ready"), sem("x_t_in_psum"), sem("x_t_copied"),
                                                  sem("gate_activated"), sem("hidden_ready"))
        s_th, s_thc, s_dna, s_dnd = (sem("hidden_t_in_psum"), sem("hidden_t_copied"),
                                           sem("down_copied_act"), sem("down_copied_dve"))
        with ExitStack() as st:
            xg, x_t, y_e = ([big[:, 11456 + 2048 * a + 1024 * i:12480 + 2048 * a + 1024 * i] for i in range(2)] for a in range(3))
            idx = [sb(f"idx{i}", [P, 1], I32, stack=st) for i in range(2)]
            sil = [sb(f"sil{i}", [P, FF], stack=st) for i in range(2)]
            hid = [sb(f"hid{i}", [P, FF], stack=st) for i in range(2)]
            hid_t = [sb(f"hid_t{i}", [P, 2, P], stack=st) for i in range(2)]

            with nc.Block() as block:
                @block.sync
                def _(sp):
                    load = load_weights(sp)

                    turns = loop_turns(sp)
                    with sp.Fori(0, turns) as n:
                        load(2 * n + 2, 0, n + 1)
                        load(2 * n + 3, 1, n + 1)

                @block.gpsimd
                def _(pool):
                    def gather(b, i, guard):
                        if guard is not None:
                            pool.wait_ge(s_tx, b - 1)
                            pool.wait_ge(s_xg[i], 16 * guard)
                        nc.gpsimd.tensor_copy(idx[i][:, :], tok_i[:, bass.ds(b, 1)]).then_inc(s_ix, 1)
                        pool.wait_ge(s_ix, b + 1)
                        pool.sem_inc(s_ixs, 1)
                        nc.gpsimd.indirect_dma_start(xg[i], None, scratch["h2_rows"],
                                                     bass.IndirectOffsetOnAxis(ap=idx[i][:, 0:1], axis=0)).then_inc(s_xg[i], 16)

                    gather(0, 0, None)
                    gather(1, 1, None)
                    turns = loop_turns(pool)
                    with pool.Fori(0, turns) as n:
                        gather(2 * n + 2, 0, n + 1)
                        gather(2 * n + 3, 1, n + 1)

                @block.tensor
                def _(pe):
                    T_ = nc.tensor

                    def turn_x(b, i, h):
                        pe.wait_ge(s_xg[i], 16 * (h + 1))
                        if not isinstance(b, int) or b >= 1:
                            pe.wait_ge(s_txc, b)
                        for k in range(KT):
                            m = T_.transpose(bank[2 + k // 4][:, (k % 4) * P:(k % 4 + 1) * P], xg[i][:, k * P:(k + 1) * P], ident[:, :])
                        m.then_inc(s_tx, 1)

                    def gate_up(b, i, h):
                        pe.wait_ge(s_txc, b + 1)
                        pe.wait_ge(s_wgu[i], 32 * (h + 1))
                        if not isinstance(b, int) or b >= 2:
                            pe.wait_ge(s_hid, b - 1)
                        for k in range(KT):
                            m = T_.matmul(bank[i], x_t[i][:, k * P:(k + 1) * P], w_gu[i][:, k, :], start=(k == 0), stop=(k == KT - 1))
                        m.then_inc(s_gup, 1)

                    def turn_hid(b, i):
                        pe.wait_ge(s_hid, b + 1)
                        if not isinstance(b, int) or b >= 1:
                            pe.wait_ge(s_thc, b)
                        for k in range(2):
                            m = T_.transpose(bank[6][:, k * P:(k + 1) * P], hid[i][:, k * P:(k + 1) * P], ident[:, :])
                        m.then_inc(s_th, 1)

                    def down(b, i, h):
                        pe.wait_ge(s_thc, b + 1)
                        pe.wait_ge(s_wdn[i], 16 * (h + 1))
                        if not isinstance(b, int) or b >= 1:
                            pe.wait_ge(s_dna, b)
                            pe.wait_ge(s_dnd, b)
                        for f in range(2):
                            for k in range(2):
                                m = T_.matmul(bank[4 + f], hid_t[i][:, k, :], w_dn[i][:, k, f * 512:(f + 1) * 512], start=(k == 0), stop=(k == 1))
                        m.then_inc(s_dn, 1)

                    turn_x(0, 0, 0)
                    gate_up(0, 0, 0)
                    turn_x(1, 1, 0)
                    turn_hid(0, 0)
                    turns = loop_turns(pe)
                    with pe.Fori(0, turns) as n:
                        gate_up(2 * n + 1, 1, n)
                        turn_x(2 * n + 2, 0, n + 1)
                        down(2 * n, 0, n)
                        turn_hid(2 * n + 1, 1)
                        gate_up(2 * n + 2, 0, n + 1)
                        turn_x(2 * n + 3, 1, n + 1)
                        down(2 * n + 1, 1, n)
                        turn_hid(2 * n + 2, 0)
                    b = 2 * turns + 1
                    gate_up(b, 1, turns)
                    down(b - 1, 0, turns)
                    turn_hid(b, 1)
                    down(b, 1, turns)

                @block.scalar
                def _(act):
                    A = nc.scalar

                    def copy_x(b, i):
                        act.wait_ge(s_tx, b + 1)
                        if not isinstance(b, int) or b >= 2:
                            act.wait_ge(s_gup, b - 1)
                        A.activation(x_t[i].rearrange("p (a c) -> p a c", a=2), psum[:, 2:4, :], ACT.Copy).then_inc(s_txc, 1)

                    def silu(b, i):
                        act.wait_ge(s_gup, b + 1)
                        if not isinstance(b, int) or b >= 2:
                            act.wait_ge(s_hid, b - 1)
                        A.activation(sil[i][:, :], bank[i][:, 0:FF], ACT.Silu).then_inc(s_sil, 1)

                    def copy_down(b, i, h):
                        act.wait_ge(s_dn, b + 1)
                        if not isinstance(b, int) or b >= 2:
                            act.wait_ge(s_yst[i], 16 * h)
                        A.activation(y_e[i][:, 0:512], bank[4], ACT.Copy).then_inc(s_dna, 1)

                    def store(b, i):
                        act.wait_ge(s_dna, b + 1)
                        act.wait_ge(s_dnd, b + 1)
                        act.dma_start(scratch["expert_rows"][bass.ds(P * b, P), :], y_e[i]).then_inc(s_yst[i], 16)

                    copy_x(0, 0)
                    silu(0, 0)
                    copy_x(1, 1)
                    silu(1, 1)
                    copy_x(2, 0)
                    copy_down(0, 0, 0)
                    store(0, 0)
                    silu(2, 0)
                    copy_x(3, 1)
                    copy_down(1, 1, 0)
                    store(1, 1)
                    turns = loop_turns(act)
                    with act.Fori(1, turns) as n:
                        silu(2 * n + 1, 1)
                        copy_x(2 * n + 2, 0)
                        copy_down(2 * n, 0, n)
                        store(2 * n, 0)
                        silu(2 * n + 2, 0)
                        copy_x(2 * n + 3, 1)
                        copy_down(2 * n + 1, 1, n)
                        store(2 * n + 1, 1)
                    b = 2 * turns + 1
                    silu(b, 1)
                    copy_down(b - 1, 0, turns)
                    store(b - 1, 0)
                    copy_down(b, 1, turns)
                    store(b, 1)
                    for i in range(2):
                        act.wait_ge(s_yst[i], 16 * (turns + 1))
                        act.sem_inc(s_yseen, 1)

                @block.vector
                def _(dve):
                    V = nc.vector

                    def hidden(b, i):
                        dve.wait_ge(s_sil, b + 1)
                        if not isinstance(b, int) or b >= 2:
                            dve.wait_ge(s_th, b - 1)
                        V.tensor_tensor(hid[i][:, :], sil[i][:, :], bank[i][:, FF:2 * FF], ALU.mult).then_inc(s_hid, 1)

                    def copy_hid(b, i):
                        dve.wait_ge(s_th, b + 1)
                        if not isinstance(b, int) or b >= 2:
                            dve.wait_ge(s_dn, b - 1)
                        V.tensor_copy(hid_t[i][:, :, :], bank[6][:, 0:2 * P].rearrange("p (k c) -> p k c", k=2)).then_inc(s_thc, 1)

                    def copy_down(b, i, h):
                        dve.wait_ge(s_dn, b + 1)
                        if not isinstance(b, int) or b >= 2:
                            dve.wait_ge(s_yst[i], 16 * h)
                        V.tensor_copy(y_e[i][:, 512:D], bank[5]).then_inc(s_dnd, 1)

                    hidden(0, 0)
                    copy_hid(0, 0)
                    hidden(1, 1)
                    copy_down(0, 0, 0)
                    copy_hid(1, 1)
                    hidden(2, 0)
                    copy_down(1, 1, 0)
                    copy_hid(2, 0)
                    turns = loop_turns(dve)
                    with dve.Fori(1, turns) as n:
                        hidden(2 * n + 1, 1)
                        copy_down(2 * n, 0, n)
                        copy_hid(2 * n + 1, 1)
                        hidden(2 * n + 2, 0)
                        copy_down(2 * n + 1, 1, n)
                        copy_hid(2 * n + 2, 0)
                    b = 2 * turns + 1
                    hidden(b, 1)
                    copy_down(b - 1, 0, turns)
                    copy_hid(b, 1)
                    copy_down(b, 1, turns)

            G8 = 5
            s_gf, s_g1, s_mx, s_sq8, s_m8, s_rt8, s_y8, s_os8 = (sem("g_final_loaded"), [sem(f"rows_gathered{i}") for i in range(G8)],
                                                                 sem("x3_ready"), sem("x3_squares"), sem("x3_mean_square"),
                                                                 sem("x3_root"), sem("y_ready"), sem("y_stored"))
            s_mg8, s_wa, s_dve8 = sem("gathered_rows_used"), sem("first_rows_weighted"), sem("dve_chain8")
            s_ri8, s_sc8 = sem("x3_root_inverse"), sem("x3_scaled")
            gr = [[big[:, 7360 + 1024 * (2 * i + k):8384 + 1024 * (2 * i + k)] for k in range(2)] for i in range(G8)]
            sq8 = ring_all[:, 0:D]
            ss8 = sb("ss8", [P, NT], stack=st)
            g_row = row_p["gate1"]
            with nc.Block() as block:
                @block.gpsimd
                def _(pool):
                    def finish(u):
                        pool.wait_ge(s_sc8, u + 1)
                        if u == 0:
                            pool.wait_ge(s_gf, 16)
                        r = rows_of(u)
                        nc.gpsimd.tensor_tensor(x2_of(u)[0:r, :], x2_of(u)[0:r, :], g_row[0:r, :], ALU.mult).then_inc(s_y8, 1)

                    for t in range(NT):
                        r = rows_of(t)
                        if t >= G8:
                            pool.wait_ge(s_mg8, t - G8 + 1)
                        for k in range(2):
                            nc.gpsimd.indirect_dma_start(gr[t % G8][k][0:r, :], None, scratch["expert_rows"],
                                                         bass.IndirectOffsetOnAxis(ap=slot_i[0:r, k, t:t + 1], axis=0)).then_inc(s_g1[t % G8], 16)
                        if t >= 5:
                            finish(t - 5)
                    for u in range(NT - 5, NT):
                        finish(u)

                @block.sync
                def _(sp):
                    sp.dma_start(g_row, I["g_final"].rearrange("(o d) -> o d", o=1).to_broadcast([P, D])).then_inc(s_gf, 16)
                    for t in range(NT):
                        sp.wait_ge(s_y8, t + 1)
                        dst = O["y_p"][0, t * P:(t + 1) * P, :] if t < TT else O["y_s"].rearrange("b t d -> (b t) d")
                        sp.dma_start(dst, x2_of(t)[0:rows_of(t), :]).then_inc(s_os8, 16)
                    sp.wait_ge(s_os8, 16 * NT)

                @block.scalar
                def _(act):
                    def weigh(t):
                        r = rows_of(t)
                        act.wait_ge(s_g1[t % G8], 32 * (t // G8 + 1))
                        nc.scalar.activation(gr[t % G8][0][0:r, :], gr[t % G8][0][0:r, :], ACT.Copy, scale=w_top[0:r, 0, t:t + 1]).then_inc(s_wa, 1)

                    def scale(u):
                        r = rows_of(u)
                        act.wait_ge(s_ri8, u + 1)
                        nc.scalar.activation(x2_of(u)[0:r, :], x2_of(u)[0:r, :], ACT.Copy, scale=ss8[0:r, u:u + 1]).then_inc(s_sc8, 1)

                    weigh(0)
                    for t in range(NT + 2):
                        if t + 1 < NT:
                            weigh(t + 1)
                        if t < NT:
                            r = rows_of(t)
                            act.wait_ge(s_mx, t + 1)
                            if t:
                                act.wait_ge(s_sq8, t)
                            nc.scalar.activation(sq8[0:r, :], x2_of(t)[0:r, :], ACT.Square, accum_out=ss8[0:r, t:t + 1]).then_inc(s_sq8, 1)
                        if 1 <= t <= NT:
                            r = rows_of(t - 1)
                            act.wait_ge(s_m8, t)
                            nc.scalar.activation(ss8[0:r, t - 1:t], ss8[0:r, t - 1:t], ACT.Sqrt).then_inc(s_rt8, 1)
                        if t >= 2:
                            scale(t - 2)

                @block.vector
                def _(dve):
                    V = nc.vector
                    c = Counted(s_dve8)
                    for t in range(NT + 2):
                        if t < NT:
                            r = rows_of(t)
                            a, b = (g_[0:r, :] for g_ in gr[t % G8])
                            x3 = x2_of(t)[0:r, :]
                            dve.wait_ge(s_wa, t + 1)
                            dve.wait_ge(s_g1[t % G8], 32 * (t // G8 + 1))
                            c.step(dve, V.scalar_tensor_tensor(out=a, in0=b, scalar=w_top[0:r, 1, t:t + 1], in1=a, op0=ALU.mult, op1=ALU.add))
                            c.step(dve, V.tensor_tensor(a, a, (row_p if t < TT else row_s)["gate2"][0:r, :], ALU.mult))
                            c.step(dve, V.tensor_tensor(x3, x3, a, ALU.add))
                            dve.sem_inc(s_mg8, 1)
                            dve.sem_inc(s_mx, 1)
                        if 1 <= t <= NT:
                            u = t - 1
                            r = rows_of(u)
                            dve.wait_ge(s_sq8, u + 1)
                            V.tensor_scalar(ss8[0:r, u:u + 1], ss8[0:r, u:u + 1], 1.0 / D, EPS, ALU.mult, ALU.add).then_inc(s_m8, 1)
                        if t >= 2:
                            u = t - 2
                            r = rows_of(u)
                            dve.wait_ge(s_rt8, u + 1)
                            V.reciprocal(ss8[0:r, u:u + 1], ss8[0:r, u:u + 1]).then_inc(s_ri8, 1)


_OUT = [("y_p", (1, SEQ, D)), ("y_s", (DEC_B, DEC_T, D)),
        ("pk0", (1, 1, 128, HEADS, HD)), ("pv0", (1, 1, 128, HEADS, HD)),
        ("pk1", (1, 1, 512, HEADS, HD)), ("pv1", (1, 1, 512, HEADS, HD)),
        ("pk2", (1, 1, 1024, HEADS, HD)), ("pv2", (1, 1, 1024, HEADS, HD)),
        ("p_re", (1, 1, SSM_G, SSM_S)), ("p_im", (1, 1, SSM_G, SSM_S)),
        ("sk0", (1, DEC_B, DEC_T, HEADS, HD)), ("sv0", (1, DEC_B, DEC_T, HEADS, HD)),
        ("sk1", (1, DEC_B, DEC_T, HEADS, HD)), ("sv1", (1, DEC_B, DEC_T, HEADS, HD)),
        ("sk2", (1, DEC_B, DEC_T, HEADS, HD)), ("sv2", (1, DEC_B, DEC_T, HEADS, HD)),
        ("s_re", (1, DEC_B, SSM_G, SSM_S)), ("s_im", (1, DEC_B, SSM_G, SSM_S))]
_SCRATCH = [("u_new", (NS, SSM_W)), ("att_rows", (N, GROUPS, HEADS, HD + 2)), ("h2_rows", (N, D)), ("gates", (2 * KT, P, N)),
            ("expert_rows", (NBLK * P, D))]


def kernel(**inputs):
    import numpy as _np
    import concourse.bacc as _bacc
    from concourse.bass_utils import run_bass_kernel_spmd as _run

    nc = _bacc.Bacc("TRN2", target_bir_lowering=False, num_devices=1)
    arrays, ins, outs, scratch = {}, {}, {}, {}
    for name, value in inputs.items():
        a = _np.ascontiguousarray(value)
        arrays["in_" + name] = a
        ins[name] = nc.dram_tensor("in_" + name, a.shape, mybir.dt.from_np(a.dtype), kind="ExternalInput").ap()
    for name, shape in _OUT:
        outs[name] = nc.dram_tensor("out_" + name, shape, F32, kind="ExternalOutput").ap()
    for name, shape in _SCRATCH:
        scratch[name] = nc.dram_tensor("tmp_" + name, shape, F32).ap()
    build(nc, ins, outs, scratch)
    r = _run(nc, [arrays], core_ids=[0])
    return tuple(r.results[0]["out_" + name] for name, _ in _OUT)
```
